# Optimizing a Trainium2 kernel written in Bass

```python
import jax, jax.numpy as jnp
from jax import lax
import numpy as np

D_MODEL = 1024
BATCH = 1
SEQ = 1024
DEPTH = 2
DEC_BATCH = 1
DEC_SEQ = 32
PAST_LEN = 256

CHUNK = 64
N_MIXERS = 2
N_HEADS = 16
HEAD_DIM = D_MODEL // N_HEADS
PAST_CHUNKS = 8
REACH = PAST_CHUNKS * CHUNK
BAND = (PAST_CHUNKS + 1) * CHUNK
MAX_REL = 128
N_REL = 2 * MAX_REL + 1
MLP_BLOCK = 128
GMLP_WIDTH = D_MODEL
N_GROUPS = 16
GROUP_DIM = GMLP_WIDTH // N_GROUPS
D_FF = 2816
CONV_W = 3
N_A = (DEPTH + 1) // 2
N_B = DEPTH // 2
EPS = 1e-6
NEG = -1e30

kernel_name = "hybrid_chunk_band_attn_gmlp_convffn_step"

def rms_norm(x, g):
    xf = x.astype(jnp.float32)
    y = xf * lax.rsqrt(jnp.mean(xf * xf, axis=-1, keepdims=True) + EPS)
    return (y * g.astype(jnp.float32)).astype(x.dtype)

def rel_bias(table, rel):
    idx = jnp.clip(rel, -MAX_REL, MAX_REL) + MAX_REL
    return table[:, idx].astype(jnp.float32)

def qkv_heads(h, w_qkv):
    B, T, _ = h.shape
    q, k, v = jnp.split(h @ w_qkv, 3, axis=-1)
    shp = (B, T, N_HEADS, HEAD_DIM)
    return q.reshape(shp), k.reshape(shp), v.reshape(shp)

def band_attn_prompt(h, w_qkv, table, w_o):
    B, S, _ = h.shape
    nc = S // CHUNK
    q, k, v = qkv_heads(h, w_qkv)
    pad = ((0, 0), (REACH, 0), (0, 0), (0, 0))
    kpad, vpad = jnp.pad(k, pad), jnp.pad(v, pad)
    rel = jnp.arange(CHUNK)[:, None] - jnp.arange(BAND)[None, :] + REACH
    bias = rel_bias(table, rel)
    scale = HEAD_DIM ** -0.5

    def one_chunk(c):
        start = c * CHUNK
        q_c = lax.dynamic_slice_in_dim(q, start, CHUNK, axis=1)
        k_c = lax.dynamic_slice_in_dim(kpad, start, BAND, axis=1)
        v_c = lax.dynamic_slice_in_dim(vpad, start, BAND, axis=1)
        s = jnp.einsum('bqhd,bkhd->bhqk', q_c, k_c).astype(jnp.float32) * scale + bias
        valid = (start - REACH + jnp.arange(BAND)) >= 0
        s = jnp.where(valid, s, NEG)
        p = jax.nn.softmax(s, axis=-1).astype(v.dtype)
        return jnp.einsum('bhqk,bkhd->bqhd', p, v_c)

    o = lax.map(one_chunk, jnp.arange(nc))
    o = jnp.moveaxis(o, 0, 1).reshape(B, S, D_MODEL)
    keep = min(REACH, S)
    return o @ w_o, k[:, S - keep:], v[:, S - keep:]

def band_attn_sample(h, cache_k, cache_v, w_qkv, table, w_o):
    B, T, _ = h.shape
    ca = cache_k.shape[1]
    q, k, v = qkv_heads(h, w_qkv)
    k_all = jnp.concatenate([cache_k.astype(k.dtype), k], axis=1)
    v_all = jnp.concatenate([cache_v.astype(v.dtype), v], axis=1)
    qpos = PAST_LEN + jnp.arange(T)
    kpos = jnp.concatenate([PAST_LEN - ca + jnp.arange(ca), PAST_LEN + jnp.arange(T)])
    bias = rel_bias(table, qpos[:, None] - kpos[None, :])
    s = jnp.einsum('bqhd,bkhd->bhqk', q, k_all).astype(jnp.float32) * (HEAD_DIM ** -0.5) + bias
    p = jax.nn.softmax(s, axis=-1).astype(v.dtype)
    o = jnp.einsum('bhqk,bkhd->bqhd', p, v_all).reshape(B, T, D_MODEL)
    return o @ w_o, k, v

def chunk_causal_mask(n):
    pos = jnp.arange(n)
    return (pos[None, :] // CHUNK) <= (pos[:, None] // CHUNK)

def gmlp_proj(h, w_in, v_gain):
    z = jax.nn.gelu(h @ w_in, approximate=False)
    u, v = jnp.split(z, 2, axis=-1)
    return u, rms_norm(v, v_gain)

def gmlp_prompt(h, w_in, v_gain, w_s, b_s, w_out):
    B, S, _ = h.shape
    nb = S // MLP_BLOCK
    u, v = gmlp_proj(h, w_in, v_gain)
    ws = jnp.where(chunk_causal_mask(MLP_BLOCK), w_s, 0.0)
    vb = v.reshape(B, nb, MLP_BLOCK, N_GROUPS, GROUP_DIM)
    mixed = jnp.einsum('gpq,bnqgd->bnpgd', ws.astype(v.dtype), vb) + b_s.T[None, None, :, :, None].astype(v.dtype)
    return (u * mixed.reshape(B, S, GMLP_WIDTH)) @ w_out

def gmlp_sample(h, w_in, v_gain, w_s, b_s, w_out):
    B, T, _ = h.shape
    u, v = gmlp_proj(h, w_in, v_gain)
    ws = jnp.where(chunk_causal_mask(MLP_BLOCK), w_s, 0.0)[:, :T, :T]
    vb = v.reshape(B, T, N_GROUPS, GROUP_DIM)
    mixed = jnp.einsum('gpq,bqgd->bpgd', ws.astype(v.dtype), vb) + b_s[:, :T].T[None, :, :, None].astype(v.dtype)
    return (u * mixed.reshape(B, T, GMLP_WIDTH)) @ w_out, v

def conv_ffn(h, hist, w_up, conv_w, conv_b, w_down):
    a = h @ w_up
    T = a.shape[1]
    full = jnp.concatenate([hist.astype(a.dtype), a], axis=1)
    c = conv_b.astype(a.dtype)
    for j in range(CONV_W):
        c = c + full[:, j:j + T] * conv_w[j].astype(a.dtype)
    gate, val = jnp.split(c, 2, axis=-1)
    return (jax.nn.silu(gate) * val) @ w_down, full[:, -(CONV_W - 1):]

def setup_inputs(seed: int = 0) -> dict:
    key = jax.random.key(seed)
    ks = jax.random.split(key, 24)
    nrm = lambda k, shp, s: jax.random.normal(k, shp, jnp.float32) * s
    ca = min(REACH, PAST_LEN)
    return {
        "x_prompt": nrm(ks[0], (BATCH, SEQ, D_MODEL), 1.0),
        "x_sample": nrm(ks[1], (DEC_BATCH, DEC_SEQ, D_MODEL), 1.0),
        "cache_a_k": nrm(ks[2], (N_A, DEC_BATCH, ca, N_HEADS, HEAD_DIM), 1.0),
        "cache_a_v": nrm(ks[3], (N_A, DEC_BATCH, ca, N_HEADS, HEAD_DIM), 1.0),
        "state_ffn_conv": nrm(ks[4], (DEPTH, DEC_BATCH, CONV_W - 1, 2 * D_FF), 1.0),
        "ln_mix": 1.0 + nrm(ks[5], (DEPTH, D_MODEL), 0.05),
        "ln_ffn": 1.0 + nrm(ks[6], (DEPTH, D_MODEL), 0.05),
        "ln_final": 1.0 + nrm(ks[7], (D_MODEL,), 0.05),
        "a_w_qkv": nrm(ks[8], (N_A, D_MODEL, 3 * D_MODEL), D_MODEL ** -0.5),
        "a_rel_bias": nrm(ks[9], (N_A, N_HEADS, N_REL), 0.5),
        "a_w_o": nrm(ks[10], (N_A, D_MODEL, D_MODEL), D_MODEL ** -0.5),
        "b_w_in": nrm(ks[11], (N_B, D_MODEL, 2 * GMLP_WIDTH), D_MODEL ** -0.5),
        "b_v_norm": 1.0 + nrm(ks[12], (N_B, GMLP_WIDTH), 0.05),
        "b_w_s": nrm(ks[13], (N_B, N_GROUPS, MLP_BLOCK, MLP_BLOCK), MLP_BLOCK ** -0.5),
        "b_bias_s": 1.0 + nrm(ks[14], (N_B, N_GROUPS, MLP_BLOCK), 0.1),
        "b_w_out": nrm(ks[15], (N_B, GMLP_WIDTH, D_MODEL), GMLP_WIDTH ** -0.5),
        "f_w_up": nrm(ks[16], (DEPTH, D_MODEL, 2 * D_FF), D_MODEL ** -0.5),
        "f_conv_w": nrm(ks[17], (DEPTH, CONV_W, 2 * D_FF), CONV_W ** -0.5),
        "f_conv_b": nrm(ks[18], (DEPTH, 2 * D_FF), 0.02),
        "f_w_down": nrm(ks[19], (DEPTH, D_FF, D_MODEL), D_FF ** -0.5),
    }

def reference(x_prompt, x_sample, cache_a_k, cache_a_v, state_ffn_conv,
              ln_mix, ln_ffn, ln_final,
              a_w_qkv, a_rel_bias, a_w_o,
              b_w_in, b_v_norm, b_w_s, b_bias_s, b_w_out,
              f_w_up, f_conv_w, f_conv_b, f_w_down):
    xp, xs = x_prompt, x_sample
    kp_l, vp_l, ks_l, vs_l, gv_l, cp_l, cs_l = [], [], [], [], [], [], []
    for i in range(DEPTH):
        j = i // N_MIXERS
        hp = rms_norm(xp, ln_mix[i])
        hs = rms_norm(xs, ln_mix[i])
        if i % N_MIXERS == 0:
            op, kp, vp = band_attn_prompt(hp, a_w_qkv[j], a_rel_bias[j], a_w_o[j])
            os_, kn, vn = band_attn_sample(hs, cache_a_k[j], cache_a_v[j], a_w_qkv[j], a_rel_bias[j], a_w_o[j])
            kp_l.append(kp); vp_l.append(vp); ks_l.append(kn); vs_l.append(vn)
        else:
            op = gmlp_prompt(hp, b_w_in[j], b_v_norm[j], b_w_s[j], b_bias_s[j], b_w_out[j])
            os_, gv = gmlp_sample(hs, b_w_in[j], b_v_norm[j], b_w_s[j], b_bias_s[j], b_w_out[j])
            gv_l.append(gv)
        xp = xp + op
        xs = xs + os_
        hp = rms_norm(xp, ln_ffn[i])
        hs = rms_norm(xs, ln_ffn[i])
        zero_hist = jnp.zeros((xp.shape[0], CONV_W - 1, 2 * D_FF), xp.dtype)
        fp, cp = conv_ffn(hp, zero_hist, f_w_up[i], f_conv_w[i], f_conv_b[i], f_w_down[i])
        fs, cs = conv_ffn(hs, state_ffn_conv[i], f_w_up[i], f_conv_w[i], f_conv_b[i], f_w_down[i])
        cp_l.append(cp); cs_l.append(cs)
        xp = xp + fp
        xs = xs + fs
    y_prompt = rms_norm(xp, ln_final)
    y_sample = rms_norm(xs, ln_final)
    return (y_prompt, y_sample, jnp.stack(kp_l), jnp.stack(vp_l), jnp.stack(ks_l), jnp.stack(vs_l),
            jnp.stack(gv_l), jnp.stack(cp_l), jnp.stack(cs_l))


_drawn_inputs = setup_inputs


def setup_inputs(seed=0):
    import zlib

    import numpy as np

    out = dict(_drawn_inputs(seed))
    spreads = {}
    factors = {'f_conv_b': 2.792}
    for name, (base, spread) in spreads.items():
        noise = np.random.default_rng([zlib.crc32(name.encode()), seed]).standard_normal(out[name].shape)
        drawn = base * np.exp(spread * noise) if base else spread * noise
        out[name] = __import__('jax').numpy.asarray(drawn.astype(out[name].dtype))
    for name, factor in factors.items():
        out[name] = (out[name] * factor).astype(out[name].dtype)
    return out
```

```python
from contextlib import ExitStack

import concourse.bass as bass
from concourse import mybir

F32 = mybir.dt.float32
F32R = mybir.dt.float32r
ALU = mybir.AluOpType
ACT = mybir.ActivationFunctionType
AX = mybir.AxisListType

P = 128
BANK = 512
EPS = 1e-6
NEG = -1e30


def build(nc, x_prompt, x_sample, cache_a_k, cache_a_v, state_ffn_conv, ln_mix, ln_ffn, ln_final,
          a_w_qkv, a_rel_bias, a_w_o, b_w_in, b_v_norm, b_w_s, b_bias_s, b_w_out,
          f_w_up, f_conv_w, f_conv_b, f_w_down,
          y_prompt, y_sample, new_k_prompt, new_v_prompt, new_k_sample, new_v_sample,
          new_gmlp_v, new_conv_prompt, new_conv_sample):
    SEQ, D = x_prompt.shape[1:]
    DEC = x_sample.shape[1]
    DEPTH = ln_mix.shape[0]
    HEADS, HD = cache_a_k.shape[3:]
    PAST = cache_a_k.shape[2]
    NREL = a_rel_bias.shape[2]
    MAXREL = NREL // 2
    KEEP = new_k_prompt.shape[2]
    GROUPS, MB = b_w_s.shape[1:3]
    FF = f_w_down.shape[1]

    KT = D // P
    GAP = 2
    TW = SEQ + GAP + DEC
    SMP = SEQ + GAP
    CH = [(0, 352), (352, 352), (704, TW - 704)]
    NCH = len(CH)
    NB = SEQ // P
    BLOCKS = [(P * b, P) for b in range(NB)] + [(SMP, DEC)]
    CK = 64
    BAND = 9 * CK
    VAR = 3 * CK
    REV = 2 * P + CK
    PAIRS = HEADS * HD // P
    FT = FF // P
    FIT = FT // 2
    CT = 2 * FT
    SCALE = HD ** -0.5
    QSCALE = 1.0 / SCALE
    assert HD == CK and FT % 2 == 0 and KEEP == 512 and PAST == 2 * P and MB == P

    ctx = ExitStack()

    def sem(name):
        return ctx.enter_context(nc.semaphore(name))

    def hold(name, shape, dt=F32):
        return ctx.enter_context(nc.sbuf_tensor(name, shape, dt))

    x = hold("x", [P, KT, TW])
    gx_hi = hold("gx_hi", [P, KT, TW], F32R)
    gx_lo = hold("gx_lo", [P, KT, TW], F32R)
    rstd = hold("rstd", [P, TW])
    ident = hold("ident", [P, P])
    ones = hold("ones", [P, P])
    gains = hold("gains", [P, 5 * KT])
    taps = [hold(f"taps{i}", [P, 6, CT]) for i in range(DEPTH)]
    raw0 = hold("raw0", [P, 2048])
    w_hi = [hold(f"w_hi{i}", [P, 1024], F32R) for i in range(2)]
    w_lo = [hold(f"w_lo{i}", [P, 1024], F32R) for i in range(2)]
    psum = ctx.enter_context(nc.psum_tensor("psum", [P, 8, BANK], F32))

    squares = hold("squares", [P, 2, 354])
    total = hold("total", [P, TW])

    def region(*allocs):
        with ExitStack() as local:
            return [local.enter_context(nc.sbuf_tensor(*a)) for a in allocs]

    xin, par_rows = region(("xin", [P, NB + 1, D], F32), ("par_rows", [P, 7, P], F32))
    (qd0, qd1, kT0, kT1, v0, v1, p_even, p_odd, pT, stage, o_hi, o_lo, bias, rel_tab, rel_rev, kc, vc,
     kcT, kout, neg_max, row_sum, row_inv) = region(
        ("qd0", [P, SEQ // CK + 1, P], F32), ("qd1", [P, SEQ // CK + 1, P], F32),
        ("kT0", [P, TW], F32), ("kT1", [P, TW], F32),
        ("v0", [P, NB + 1, P], F32), ("v1", [P, NB + 1, P], F32),
        ("p_even", [P, 5 * P], F32), ("p_odd", [P, 5 * P], F32), ("pT", [P, 2, 4 * P], F32),
        ("stage", [P, TW], F32), ("o_hi", [P, TW], F32R), ("o_lo", [P, TW], F32R),
        ("bias", [P, PAIRS, VAR], F32), ("rel_tab", [HEADS, NREL], F32), ("rel_rev", [HEADS, REV], F32),
        ("kc", [P, 2, P], F32), ("vc", [P, 2, P], F32), ("kcT", [P, PAST], F32), ("kout", [P, 5, P], F32),
        ("neg_max", [P, 2], F32), ("row_sum", [P, 2], F32), ("row_inv", [P, 2], F32))
    qd, kT, v_tok = [qd0, qd1], [kT0, kT1], [v0, v1]
    (raw1, w_hi2, w_hi3, w_lo2, w_lo3, a_gate, a_val, s_gate, h_hiA, h_hiB, h_loA, h_loB,
     conv_t, prod, cur, tails, tails_row) = region(
        ("raw1", [P, 2048], F32), ("w_hi2", [P, 1024], F32R), ("w_hi3", [P, 1024], F32R),
        ("w_lo2", [P, 1024], F32R), ("w_lo3", [P, 1024], F32R),
        ("a_gate", [P, TW + GAP], F32), ("a_val", [P, TW + GAP], F32), ("s_gate", [P, TW], F32),
        ("h_hiA", [P, TW], F32R), ("h_hiB", [P, TW], F32R), ("h_loA", [P, TW], F32R), ("h_loB", [P, TW], F32R),
        ("conv_t", [P, 2, 354], F32), ("prod", [P, 2, 354], F32), ("cur", [P, 6, 2, 2], F32),
        ("tails", [P, 4, CT], F32), ("tails_row", [P, 2, P], F32))
    a_buf, h_hi, h_lo = [a_gate, a_val], [h_hiA, h_hiB], [h_loA, h_loB]
    final_g, y0, y1, rcol = region(("final_g", [P, D], F32), ("y0", [P, D], F32), ("y1", [P, D], F32),
                                   ("rcol", [P, NB + 1], F32))
    y_tile = [y0, y1]
    vT, vt0, vt1, wsT, bs, gain_v, gm_t, rc_v = region(
        ("vT", [P, KT, TW], F32), ("vt0", [P, KT, 2, P], F32), ("vt1", [P, KT, 2, P], F32),
        ("wsT", [P, GROUPS, P], F32), ("bs", [P, KT, P], F32), ("gain_v", [P, D], F32),
        ("gm_t", [P, 2, 354], F32), ("rc_v", [P, NB + 1], F32))
    v_pad = [vt0, vt1]
    f_hi, f_lo = w_hi + [w_hi2, w_hi3], w_lo + [w_lo2, w_lo3]
    bias_scratch = nc.dram_tensor("bias_scratch", [HEADS, CK, REV], F32, kind="Internal").ap()

    def at_least(engine, semaphore, value):
        if not isinstance(value, int) or value > 0:
            engine.wait_ge(semaphore, value)

    passed = sem("passed")

    def stand(engine):
        engine.sem_inc(passed, 1)

    def chunk(t, c):
        start, n = CH[c]
        return t[..., start:start + n]

    def product(pe, out, w, rhs, first, last):
        pe.matmul(out, w[0], rhs[0], start=first, stop=False)
        pe.matmul(out, w[0], rhs[1], start=False, stop=False)
        return pe.matmul(out, w[1], rhs[0], start=False, stop=last)

    def linear(pe, out, hi, lo, c):
        for k in range(KT):
            cut = slice(k * P, (k + 1) * P)
            last = product(pe, out, (hi[:, cut], lo[:, cut]), (chunk(gx_hi[:, k, :], c), chunk(gx_lo[:, k, :], c)),
                           k == 0, k == KT - 1)
        return last

    def psum_pair(first_bank, n):
        if n <= BANK:
            return psum[:, first_bank, :n]
        return psum[:, first_bank:first_bank + 2, :n // 2]

    class Norm:

        def __init__(self, index, which, x_ready, split=True, bank=7):
            self.bank = bank
            self.which, self.x_ready, self.split = which, x_ready, split
            self.tiles, self.chunks = KT * NCH * index, NCH * index

        hi = sem("norm_hi")
        lo = sem("norm_lo")
        squared = sem("norm_squared")
        added = sem("norm_added")
        summed = sem("norm_summed")
        mean = sem("norm_mean")
        root = sem("norm_root")
        ready = sem("norm_rstd")

        def gain(self, d):
            return gains[:, self.which * KT + d:self.which * KT + d + 1]

        def act_tile(self, act, c, d):
            k = KT * c + d
            self.x_ready(act, c, d)
            src = chunk(x[:, d, :], c)
            if self.split:
                act.activation(chunk(gx_hi[:, d, :], c), src, ACT.Copy, scale=self.gain(d)).then_inc(self.hi, 1)
            at_least(act, self.added, self.tiles + k - 1)
            act.activation(squares[:, k % 2, :CH[c][1]], src, ACT.Square).then_inc(self.squared, 1)

        def dve_tile(self, dve, c, d):
            if self.split:
                dve.wait_ge(self.hi, self.tiles + KT * c + d + 1)
                dve.scalar_tensor_tensor(chunk(gx_lo[:, d, :], c), chunk(x[:, d, :], c), self.gain(d),
                                         chunk(gx_hi[:, d, :], c), ALU.mult, ALU.subtract).then_inc(self.lo, 1)

        def pool(self, pool, c):
            for d in range(KT):
                k = KT * c + d
                pool.wait_ge(self.squared, self.tiles + k + 1)
                sq = squares[:, k % 2, :CH[c][1]]
                if d == 0:
                    pool.tensor_copy(chunk(total, c), sq).then_inc(self.added, 1)
                else:
                    pool.wait_ge(self.added, self.tiles + k)
                    pool.tensor_tensor(chunk(total, c), chunk(total, c), sq, ALU.add).then_inc(self.added, 1)

        def pe_sum(self, pe, c):
            pe.wait_ge(self.added, self.tiles + KT * (c + 1))
            at_least(pe, self.mean, self.chunks + c)
            pe.matmul(psum[:, self.bank, :CH[c][1]], ones[:, :], chunk(total, c), start=True, stop=True)\
                .then_inc(self.summed, 1)

        def dve_mean(self, dve, c):
            dve.wait_ge(self.summed, self.chunks + c + 1)
            dve.tensor_scalar(chunk(rstd, c), psum[:, self.bank, :CH[c][1]], 1.0 / D, EPS, ALU.mult, ALU.add)\
                .then_inc(self.mean, 1)

        def act_root(self, act, c):
            act.wait_ge(self.mean, self.chunks + c + 1)
            act.activation(chunk(rstd, c), chunk(rstd, c), ACT.Sqrt).then_inc(self.root, 1)

        def dve_rstd(self, dve, c):
            dve.wait_ge(self.root, self.chunks + c + 1)
            dve.reciprocal(chunk(rstd, c), chunk(rstd, c)).then_inc(self.ready, 1)

        def dve_row(self, dve, c):
            self.dve_mean(dve, c)
            self.dve_rstd(dve, c)
            dve.wait_ge(self.ready, self.chunks + c + 1)

    x_in = [sem(f"x_in{b}") for b in range(NB + 1)]
    par_in = sem("par_in")
    consts = sem("consts")
    x_turned = sem("x_turned")
    x_act = sem("x_act")
    x_dve = sem("x_dve")
    par_turned = sem("par_turned")
    par_done = sem("par_done")
    LAST_BLOCK = [max(b for b in range(NB + 1) if BLOCKS[b][0] < CH[c][0] + CH[c][1]) for c in range(NCH)]
    PAR_ROWS = [5 * KT] + [2 * CT] * (3 * DEPTH)

    def x0_ready(engine, c, d):
        engine.wait_ge(x_act, LAST_BLOCK[c] + 1)
        engine.wait_ge(x_dve, LAST_BLOCK[c] + 1)
        if c == 0 and d == 0:
            engine.wait_ge(consts, 4)
            engine.wait_ge(par_done, 1)

    norm_a = Norm(0, 0, x0_ready, bank=4)

    def input_sp(sp):
        for b in range(0, NB, 2):
            sp.dma_start(xin[:, b, :], x_prompt[0, P * b:P * (b + 1), :]).then_inc(x_in[b], 16)
        sp.dma_start(xin[:DEC, NB, :], x_sample[0]).then_inc(x_in[NB], 16)

    def input_act_dma(act):
        act.dma_start(par_rows[:2 * KT, 0, :], ln_mix.rearrange("l (t p) -> (l t) p", p=P)).then_inc(par_in, 16)
        act.dma_start(par_rows[2 * KT:4 * KT, 0, :], ln_ffn.rearrange("l (t p) -> (l t) p", p=P)).then_inc(par_in, 16)
        act.dma_start(par_rows[4 * KT:5 * KT, 0, :], ln_final.rearrange("(t p) -> t p", p=P)).then_inc(par_in, 16)
        for b in range(1, NB, 2):
            act.dma_start(xin[:, b, :], x_prompt[0, P * b:P * (b + 1), :]).then_inc(x_in[b], 16)
        for i in range(DEPTH):
            act.dma_start(par_rows[:2 * CT, 1 + 3 * i, :],
                          f_conv_w[i, 0:2].rearrange("j (t p) -> (j t) p", p=P)).then_inc(par_in, 16)
            act.dma_start(par_rows[:CT, 2 + 3 * i, :],
                          f_conv_w[i, 2].rearrange("(t p) -> t p", p=P)).then_inc(par_in, 16)
            act.dma_start(par_rows[CT:2 * CT, 2 + 3 * i, :],
                          f_conv_b[i].rearrange("(t p) -> t p", p=P)).then_inc(par_in, 16)
            act.dma_start(par_rows[:2 * CT, 3 + 3 * i, :],
                          state_ffn_conv[i, 0].rearrange("j (t p) -> (j t) p", p=P)).then_inc(par_in, 16)

    PAR_DMAS = 3 + 4 * DEPTH

    def input_pool(pool):
        pool.memset(ident[:, :], 0.0).then_inc(consts, 1)
        pool.wait_ge(consts, 1)
        pool.affine_select(out=ident[:, :], in_=ident[:, :], compare_op=ALU.not_equal, fill=1.0, base=0,
                           pattern=[[-1, P]], channel_multiplier=1).then_inc(consts, 1)
        pool.memset(ones[:, :], 1.0).then_inc(consts, 1)
        pool.memset(x[:, :, SEQ:SMP], 0.0).then_inc(consts, 1)

    def turn_block(pe, b):
        n = BLOCKS[b][1]
        pe.wait_ge(x_in[b], 16)
        for half in range(2):
            at_least(pe, (x_act, x_dve)[half], b - 1)
            for j in range(4):
                d = 4 * half + j
                last = pe.transpose(psum[:, half + 2 * (b % 2), j * P:j * P + n],
                                    xin[:n, b, d * P:(d + 1) * P], ident[:n, :n])
            last.then_inc(x_turned, 1)

    def turned(b, half):
        start, n = BLOCKS[b]
        src = psum[:, half + 2 * (b % 2), :].rearrange("p (j n) -> p j n", j=4)[:, :, :n]
        return x[:, 4 * half:4 * half + 4, start:start + n], src

    def turn_params(pe, i):
        pe.wait_ge(par_in, 16 * PAR_DMAS)
        pe.wait_ge(consts, 2)
        at_least(pe, par_done, i)
        n = PAR_ROWS[i]
        pe.transpose(psum[:, 5, :n], par_rows[:n, i, :], ident[:n, :n]).then_inc(par_turned, 1)

    def copy_params(act, i):
        act.wait_ge(par_turned, i + 1)
        n = PAR_ROWS[i]
        if i == 0:
            dst, src = gains[:, :], psum[:, 5, :n]
        else:
            layer, part = divmod(i - 1, 3)
            dst = taps[layer][:, 2 * part:2 * part + 2, :]
            src = psum[:, 5, :n].rearrange("p (j t) -> p j t", j=2)
        act.activation(dst, src, ACT.Copy).then_inc(par_done, 1)

    def input_pe(pe):
        turn_params(pe, 0)
        for b in range(NB + 1):
            turn_block(pe, b)
            if b == 5:
                for i in range(1, 4):
                    turn_params(pe, i)
                norm_a.pe_sum(pe, 0)
        for i in range(4, len(PAR_ROWS)):
            turn_params(pe, i)
        norm_a.pe_sum(pe, 1)

    def input_act(act):
        copy_params(act, 0)
        split_act(act, 0)
        split_act(act, 1)
        for b in range(NB + 1):
            act.wait_ge(x_turned, 2 * b + 1)
            act.activation(*turned(b, 0), ACT.Copy).then_inc(x_act, 1)
            if b in LAST_BLOCK:
                c = LAST_BLOCK.index(b)
                for d in range(KT):
                    norm_a.act_tile(act, c, d)
                if c == 1:
                    for i in range(1, 4):
                        copy_params(act, i)
                    norm_a.act_root(act, 0)
        for i in range(4, len(PAR_ROWS)):
            copy_params(act, i)
        norm_a.act_root(act, 1)

    def input_dve(dve):
        split_dve(dve, 0)
        split_dve(dve, 1)
        for b in range(NB + 1):
            dve.wait_ge(x_turned, 2 * b + 2)
            dve.tensor_copy(*turned(b, 1)).then_inc(x_dve, 1)
            if b in LAST_BLOCK:
                c = LAST_BLOCK.index(b)
                for d in range(KT):
                    norm_a.dve_tile(dve, c, d)
                if c == 1:
                    norm_a.dve_row(dve, 0)
        norm_a.dve_row(dve, 1)

    QKV0 = 3
    at_raw = [sem(f"at_raw{i}") for i in range(2)]
    at_hi = sem("at_hi")
    at_lo = sem("at_lo")
    qkv_done = sem("qkv_done")
    oq_free = sem("oq_free")
    qk_done = sem("qk_done")
    masked = sem("biased")
    max_done = sem("max_done")
    exp_done = sem("exp_done")
    inv_done = sem("inv_done")
    p_done = sem("p_done")
    t_done = sem("t_done")
    t_free = sem("t_free")
    pv_done = sem("pv_done")
    o_hi_done = sem("o_hi_done")
    wo_done = sem("wo_done")
    at_added = sem("at_added")
    at_zero = sem("at_zero")
    p_zero = sem("p_zero")
    rel_in = sem("rel_in")
    rel_done = sem("rel_done")
    rel_out = sem("rel_out")
    bias_in = sem("bias_in")
    kc_in = sem("kc_in")
    vc_in = sem("vc_in")
    k_out = sem("k_out")
    v_out = sem("v_out")

    STEPS = NB + 1
    BURST = NCH * KT

    def key_blocks(s):
        return list(range(max(0, s - 4), s + 1)) if s < NB else list(range(3))

    def key_groups(s):
        blocks = key_blocks(s)
        return [blocks[i:i + 2] for i in range(0, len(blocks), 2)]

    PV_PAIR = sum(len(key_groups(s)) for s in range(STEPS))
    EXTRAS = {0: [("kc",)], 3: [("v", 0, 1, 2, 3)], 4: [("v", 4, 5, 6, 7)], 5: [("v", 8)],
              6: [("k", 4, 5, 6, 7)], 7: [("k", 8)]}
    T_FIRST = sum(len(e) for e in EXTRAS.values()) - 1
    V_FIRST = sum(len(EXTRAS[s]) for s in (3, 4, 5))
    T_PAIR = PV_PAIR + T_FIRST + 1
    assert T_PAIR % 2 == 0

    def extras(s, cached, following):
        return [e for e in EXTRAS.get(s, []) if (cached if e[0] == "kc" else following)]

    class Plan:

        def __init__(self, following):
            self.oq, self.o, self.q, n = [], {}, {}, 0
            for s in range(STEPS + 1):
                if s:
                    self.o[s - 1] = n
                    n += 1
                if s < STEPS and following:
                    self.q[s] = n
                    n += 1
            self.n_oq = n
            self.t, self.extra, self.pv, n, m, users = {}, {}, {}, 0, 0, {}
            for s in range(STEPS + 1):
                if s:
                    for g in range(len(key_groups(s - 1))):
                        slot = (T_FIRST + n) % 2
                        self.t[s - 1, g] = (n, m, users.get(slot, 0))
                        users[slot] = m + 1
                        n, m = n + 1, m + 1
                if s < STEPS:
                    for e in extras(s, True, following):
                        self.extra[s, e] = n
                        n += 1

    PLAN = {f: Plan(f) for f in (False, True)}
    OQ_FIRST, OQ_PAIR = STEPS, PLAN[True].n_oq
    assert OQ_PAIR % 2 == 0

    def chunk_scores(s, odd):
        if s == NB:
            return 0, PAST + DEC
        c = 2 * s + odd
        return CK * max(0, c - 8), CK * (min(c, 8) + 1)

    def scores_of(s, odd):
        return psum_pair(2 * odd, chunk_scores(s, odd)[1])

    def chunks_of(s):
        return [0, 1] if s < NB else [0]

    def split_act(act, n):
        act.wait_ge(at_raw[n % 2], 16 * (n // 2 + 1))
        act.activation(w_hi[n % 2][:, :], raw0[:, 1024 * (n % 2):1024 * (n % 2) + 1024], ACT.Copy).then_inc(at_hi, 1)

    def split_dve(dve, n):
        dve.wait_ge(at_hi, n + 1)
        dve.tensor_tensor(w_lo[n % 2][:, :], raw0[:, 1024 * (n % 2):1024 * (n % 2) + 1024], w_hi[n % 2][:, :],
                          ALU.subtract).then_inc(at_lo, 1)

    class Unit:

        def __init__(self, t, par, k):
            self.slot = (QKV0 + 4 * par + k) % 2
            self.count = QKV0 + 4 * t + k + 1
            self.loads = 2 * t + (QKV0 + k) // 2 + 1

        def act(self, act):
            act.wait_ge(at_raw[self.slot], 16 * self.loads)
            act.activation(w_hi[self.slot][:, :], raw0[:, 1024 * self.slot:1024 * self.slot + 1024], ACT.Copy)\
                .then_inc(at_hi, 1)

        def dve(self, dve):
            dve.wait_ge(at_hi, self.count)
            dve.tensor_tensor(w_lo[self.slot][:, :], raw0[:, 1024 * self.slot:1024 * self.slot + 1024],
                              w_hi[self.slot][:, :], ALU.subtract).then_inc(at_lo, 1)

    def load_unit(sp, n_mod, count, src):
        at_least(sp, at_lo, count - 2)
        if not isinstance(count, int):
            stand(sp)
        raw = raw0[:, 1024 * n_mod:1024 * n_mod + 1024]
        if src.shape[0] != P:
            src = src.rearrange("(k p) n -> p k n", p=P)
            raw = raw.rearrange("p (k n) -> p k n", k=KT)
        sp.dma_start(raw, src).then_inc(at_raw[n_mod], 16)

    def qkv_unit(which, t):
        return a_w_qkv[0, :, bass.ds(D * which + P * t, P)]

    def attention_sp(sp):
        def pair(t, par, units):
            for k in units:
                src = {0: lambda: qkv_unit(2, t + 1), 1: lambda: qkv_unit(1, t + 1), 2: lambda: qkv_unit(0, t + 1),
                       3: lambda: a_w_o[0, bass.ds(P * t, P), :], 4: lambda: qkv_unit(2, t + 2)}[k]()
                load_unit(sp, (QKV0 + k) % 2, QKV0 + 4 * t + k + 1, src)

        load_unit(sp, QKV0 % 2, QKV0 + 1, qkv_unit(2, 1))
        with sp.Fori(0, PAIRS // 2 - 1) as j:
            pair(2 * j, 0, [1, 2, 3, 4])
            pair(2 * j + 1, 1, [1, 2, 3, 4])
        pair(PAIRS - 2, 0, [1, 2, 3])
        load_unit(sp, (QKV0 + 4) % 2, QKV0 + 4 * (PAIRS - 2) + 5, a_w_o[0, P * (PAIRS - 1):, :])

    def attention_first_sp(sp):
        for n, which in enumerate([2, 1]):
            load_unit(sp, n, n + 1, qkv_unit(which, 0))

    def attention_second_sp(sp):
        load_unit(sp, 0, 3, qkv_unit(0, 0))

    def attention_pool(pool):
        pool.wait_ge(x_act, NB + 1)
        pool.wait_ge(x_dve, NB + 1)
        pool.wait_ge(par_done, len(PAR_ROWS))
        pool.dma_start(rel_tab[:, :], a_rel_bias[0]).then_inc(rel_in, 16)
        pool.memset(rel_rev[:, 0:P], 0.0).then_inc(rel_done, 1)
        for t in (qd0, qd1):
            pool.memset(t[:, :, :], 0.0).then_inc(at_zero, 1)
        pool.memset(p_even[:, BAND:], 0.0).then_inc(at_zero, 1)
        pool.memset(p_odd[:, :CK], 0.0).then_inc(at_zero, 1)
        for t in (o_hi, o_lo):
            pool.memset(t[:, SEQ:SMP].bitcast(F32), 0.0).then_inc(at_zero, 1)
        pool.wait_ge(rel_done, 2)
        pool.dma_start(bias_scratch, rel_rev[:, None, :].to_broadcast([HEADS, CK, REV])).then_inc(rel_out, 16)
        pool.wait_ge(rel_out, 16)
        for h in range(2):
            src = bass.AP(bias_scratch.tensor, CK * REV * h + P - 1, [[REV - 1, CK], [2 * CK * REV, PAIRS], [1, VAR]])
            pool.dma_start(bias[CK * h:CK * (h + 1), :, :], src).then_inc(bias_in, 16)

        def load_cache(t):
            for src, dst, done in ((cache_a_k, kc, kc_in), (cache_a_v, vc, vc_in)):
                flat = src[0, 0].rearrange("(b p) h e -> p b (h e)", p=P)
                pool.dma_start(dst[:, :, :], flat[:, :, bass.ds(P * t, P)]).then_inc(done, 16)

        def store(t, par, t_count, v_count):
            if v_count is not None:
                pool.wait_ge(t_free, v_count)
                stand(pool)
                pool.dma_start(new_v_prompt[0, 0].rearrange("(b p) h e -> p b (h e)", p=P)[:, :, bass.ds(P * t, P)],
                               v_tok[par][:, NB - 4:NB, :]).then_inc(v_out, 16)
                pool.dma_start(new_v_sample[0, 0].rearrange("p h e -> p (h e)")[:, bass.ds(P * t, P)],
                               v_tok[par][:DEC, NB, :]).then_inc(v_out, 16)
            pool.wait_ge(t_free, t_count)
            stand(pool)
            pool.dma_start(new_k_prompt[0, 0].rearrange("(b p) h e -> p b (h e)", p=P)[:, :, bass.ds(P * t, P)],
                           kout[:, :4, :]).then_inc(k_out, 16)
            pool.dma_start(new_k_sample[0, 0].rearrange("p h e -> p (h e)")[:, bass.ds(P * t, P)],
                           kout[:DEC, 4, :]).then_inc(k_out, 16)

        load_cache(0)
        store(0, 0, 2 + T_FIRST, 2 + V_FIRST)

        def pair(t, par, following):
            plan = PLAN[following]
            base = T_FIRST + T_PAIR * t
            for s in range(4):
                pool.wait_ge(qk_done, (2 * NB + 1) * t + 2 * s + 1)
                stand(pool)
                pool.memset(p_even[:, P * s + CK:P * (s + 1)], 0.0).then_inc(p_zero, 1)
            if following:
                store(t + 1, 1 - par, 2 + base + plan.extra[7, ("k", 8)] + 1, 2 + base + plan.extra[5, ("v", 8)] + 1)
                pool.wait_ge(pv_done, 1 + PV_PAIR * (t + 1))
                stand(pool)
                load_cache(t + 1)

        with pool.Fori(0, PAIRS // 2 - 1) as j:
            pair(2 * j, 0, True)
            pair(2 * j + 1, 1, True)
        pair(PAIRS - 2, 0, True)
        pair(PAIRS - 1, 1, False)

    def extra_pe(pe, e, par_next, slot):
        out = psum[:, 4 + slot, :]
        for j, b in enumerate(e[1:] if e[0] != "kc" else (0, 1)):
            if e[0] == "kc":
                last = pe.transpose(out[:, P * j:P * (j + 1)], kc[:, b, :], ident[:, :])
            else:
                start, n = BLOCKS[b]
                src = stage if e[0] == "v" else kT[par_next]
                last = pe.transpose(out[:n, P * j:P * (j + 1)], src[:, start:start + n], ident[:, :])
        last.then_inc(t_done, 1)

    def extra_act(act, e, par_next, slot):
        out = psum[:, 4 + slot, :]
        if e[0] == "kc":
            dst, src = kcT[:, :], out[:, :PAST]
        else:
            first, n, m = e[1], BLOCKS[e[1]][1], len(e) - 1
            src = out[:n, :P * m].rearrange("p (b n) -> p b n", n=P)
            dst = v_tok[par_next][:n, first:first + m, :] if e[0] == "v" else kout[:n, first - 4:first - 4 + m, :]
        act.activation(dst, src, ACT.Copy).then_inc(t_free, 1)

    def qkv_pe(pe, u, c, bank, unit_count, slot):
        pe.wait_ge(at_lo, unit_count)
        linear(pe, psum[:, bank, :CH[c][1]], w_hi[slot], w_lo[slot], c).then_inc(qkv_done, 1)

    def attention_pe(pe):
        for o in range(STEPS):
            u, c = divmod(o, NCH)
            if u == 0:
                pe.wait_ge(norm_a.lo, KT * (c + 1))
            if o == 2:
                norm_a.pe_sum(pe, 2)
            pe.wait_ge(oq_free, o + 1)
            qkv_pe(pe, u, c, 6 + o % 2, u + 1, u % 2)
            if o == 5:
                pe.wait_ge(oq_free, 2 + 3)
                for n, e in enumerate([e for s in (3, 4, 5) for e in EXTRAS[s]]):
                    pe.wait_ge(t_free, n + 1)
                    extra_pe(pe, e, 0, n % 2)
        pe.wait_ge(oq_free, 2 + 6)
        for n, e in enumerate([e for s in (6, 7) for e in EXTRAS[s]]):
            pe.wait_ge(t_free, V_FIRST + n + 1)
            extra_pe(pe, e, 0, (V_FIRST + n) % 2)

        def values(t, par, s, plan):
            bank = 6 + (OQ_FIRST + plan.o[s]) % 2
            blocks = key_blocks(s)
            pe.wait_ge(p_done, (2 * NB + 1) * t + 2 * s + len(chunks_of(s)))
            if s < 4:
                pe.wait_ge(p_zero, 4 * t + s + 1)

            def turn(g, group):
                n, m, _ = plan.t[s, g]
                slot = (T_FIRST + n) % 2
                pe.wait_ge(t_free, T_FIRST + T_PAIR * t + n + 1)
                for i, kb in enumerate(group):
                    rows = P if s < NB or kb < 2 else DEC
                    for odd in chunks_of(s):
                        at = P * (kb - blocks[0]) + (CK if odd and s < 4 else 0)
                        src = (p_even, p_odd)[odd][:, at:at + rows]
                        last = pe.transpose(psum[:rows, 4 + slot, P * (2 * i + odd):P * (2 * i + odd + 1)],
                                            src, ident[:, :])
                last.then_inc(t_done, 1)

            def weigh(g, group):
                n, m, _ = plan.t[s, g]
                slot = (T_FIRST + n) % 2
                width = 2 * P if s < NB else P
                pe.wait_ge(t_free, 2 + T_FIRST + T_PAIR * t + n + 1)
                if g == 0:
                    pe.wait_ge(oq_free, OQ_FIRST + OQ_PAIR * t + plan.o[s] + 1)
                    if s == NB:
                        pe.wait_ge(vc_in, 16 * (t + 1))
                for i, kb in enumerate(group):
                    rows = P if s < NB or kb < 2 else DEC
                    v = v_tok[par][:rows, kb if s < NB else NB, :] if s < NB or kb == 2 else vc[:, kb, :]
                    mm = pe.matmul(psum[:, bank, :width], v, pT[:rows, slot, 2 * P * i:2 * P * i + width],
                                   start=(kb == blocks[0]), stop=(kb == blocks[-1]))
                mm.then_inc(pv_done, 1)

            groups = key_groups(s)
            ahead = 1
            for g in range(len(groups) + ahead):
                if g < len(groups):
                    turn(g, groups[g])
                if g >= ahead:
                    weigh(g - ahead, groups[g - ahead])

        def pair(t, par, following):
            plan = PLAN[following]
            base = T_FIRST + T_PAIR * t
            pe.wait_ge(oq_free, 2 + OQ_PAIR * t + OQ_FIRST)
            pe.wait_ge(at_added, BURST * t + 1)
            for s in range(STEPS + 1):
                if s:
                    values(t, par, s - 1, plan)
                if s == STEPS:
                    break
                for odd in chunks_of(s):
                    q = (2 * NB + 1) * t + 2 * s + odd
                    if s:
                        pe.wait_ge(exp_done, (2 * NB + 1) * t + 2 * (s - 1) + odd + 1)
                    first, n = chunk_scores(s, odd)
                    stat = qd[par][:, 2 * s + odd, :]
                    if s == NB:
                        pe.wait_ge(t_free, 2 + base + plan.extra[0, ("kc",)] + 1)
                        pe.matmul(psum[:, 0, :PAST], stat, kcT[:, :], start=True, stop=True)
                        last = pe.matmul(psum[:, 0, PAST:n], stat, kT[par][:, SMP:], start=True, stop=True)
                    elif n <= BANK:
                        last = pe.matmul(psum[:, 2 * odd, :n], stat, kT[par][:, first:first + n], start=True, stop=True)
                    else:
                        for i in range(2):
                            last = pe.matmul(psum[:, 2 * odd + i, :n // 2], stat,
                                             kT[par][:, first + i * n // 2:first + (i + 1) * n // 2],
                                             start=True, stop=True)
                    last.then_inc(qk_done, 1)
                if following:
                    u, c = divmod(s, NCH)
                    k = OQ_FIRST + plan.q[s]
                    pe.wait_ge(oq_free, OQ_PAIR * t + k + 1)
                    qkv_pe(pe, u, c, 6 + k % 2, QKV0 + 4 * t + u + 1, (QKV0 + u) % 2)
                for e in extras(s, True, following):
                    n = plan.extra[s, e]
                    pe.wait_ge(t_free, base + n + 1)
                    if e[0] == "kc":
                        pe.wait_ge(kc_in, 16 * (t + 1))
                    elif e[0] == "v" and s == 3:
                        pe.wait_ge(oq_free, 2 + OQ_FIRST + OQ_PAIR * t + plan.q[2] + 1)
                    elif s == 6:
                        pe.wait_ge(oq_free, 2 + OQ_FIRST + OQ_PAIR * t + plan.q[5] + 1)
                    extra_pe(pe, e, 1 - par, (T_FIRST + n) % 2)
            k = 3 if following else 0
            slot = (QKV0 + k) % 2
            pe.wait_ge(at_lo, QKV0 + 4 * t + k + 1)
            for n in range(BURST):
                c, d = divmod(n, KT)
                if d == 0:
                    pe.wait_ge(oq_free, 2 + OQ_FIRST + OQ_PAIR * t + plan.o[LAST_BLOCK[c]] + 1)
                if n >= 4:
                    pe.wait_ge(at_added, BURST * t + n - 3 + 1)
                cut = slice(P * d, P * (d + 1))
                product(pe, psum[:, n % 4, :CH[c][1]], (w_hi[slot][:, cut], w_lo[slot][:, cut]),
                        (chunk(o_hi[:, :], c), chunk(o_lo[:, :], c)), True, True).then_inc(wo_done, 1)

        with pe.Fori(0, PAIRS // 2 - 1) as j:
            pair(2 * j, 0, True)
            pair(2 * j + 1, 1, True)
        pair(PAIRS - 2, 0, True)
        pair(PAIRS - 1, 1, False)

    def o_halves(s, tensor, par_bank):
        start, n = BLOCKS[s]
        for h in range(2):
            rows = slice(CK * h, CK * (h + 1))
            if s < NB:
                dst = tensor[rows, start:start + n].rearrange("p (c q) -> p c q", q=CK)
                src = psum[rows, par_bank, :2 * P].rearrange("p (c h q) -> p c h q", h=2, q=CK)[:, :, h, :]
            else:
                dst = tensor[rows, start:start + n]
                src = psum[rows, par_bank, CK * h:CK * h + DEC]
            yield dst, src

    def attention_act(act, norm):
        norm_a.act_root(act, 2)
        act.wait_ge(qkv_done, 3)
        split_act(act, 2)
        act.wait_ge(qkv_done, 6)
        split_act(act, 3)
        firsts = [e for s in (3, 4, 5, 6, 7) for e in EXTRAS[s]]
        for n, e in enumerate(firsts):
            act.wait_ge(t_done, n + 1)
            extra_act(act, e, 0, n % 2)

        def pair(half, par, following, again):
            t = 2 * half + par
            plan = PLAN[following]
            base = T_FIRST + T_PAIR * t
            tiles = (2 * NB + 1) * t
            for s in range(STEPS + 1):
                if s:
                    groups = key_groups(s - 1)
                    for g, group in enumerate(groups):
                        n, m, before = plan.t[s - 1, g]
                        slot = (T_FIRST + n) % 2
                        rows = P if s - 1 < NB or group[0] < 2 else DEC
                        width = 2 * P if s - 1 < NB else P
                        act.wait_ge(t_done, base + n + 1)
                        act.wait_ge(pv_done, 1 + PV_PAIR * t + before)
                        dst, src = (v[:rows].rearrange("p (i n) -> p i n", i=2)[:, :len(group), :width]
                                    for v in (pT[:, slot, :], psum[:, 4 + slot, :]))
                        act.activation(dst, src, ACT.Copy).then_inc(t_free, 1)
                    bank = 6 + (OQ_FIRST + plan.o[s - 1]) % 2
                    act.wait_ge(pv_done, 1 + PV_PAIR * t + plan.t[s - 1, len(groups) - 1][1] + 1)
                    for dst, src in o_halves(s - 1, o_hi, bank):
                        act.activation(dst, src, ACT.Copy).then_inc(o_hi_done, 1)
                if s == STEPS:
                    break
                if s == 0:
                    act.wait_ge(wo_done, BURST * t + 1)
                    act.wait_ge(qkv_done, STEPS * (t + 1))
                    Unit(t, par, 1 if following else 0).act(act)
                elif following and s == 3:
                    act.wait_ge(qkv_done, STEPS * (t + 1) + 3)
                    Unit(t, par, 2).act(act)
                elif following and s == 6:
                    act.wait_ge(qkv_done, STEPS * (t + 1) + 6)
                    Unit(t, par, 3).act(act)
                for odd in chunks_of(s):
                    q = 2 * s + odd
                    first, n = chunk_scores(s, odd)
                    act.wait_ge(max_done, tiles + q + 1)
                    dst = p_even[:, :n] if not odd else p_odd[:, CK:CK + n]
                    if n > BANK:
                        dst = dst.rearrange("p (i n) -> p i n", i=2)
                    act.activation(dst, scores_of(s, odd), ACT.Exp, bias=neg_max[:, odd:odd + 1],
                                   accum_out=row_sum[:, odd:odd + 1]).then_inc(exp_done, 1)
                for e in extras(s, True, following):
                    n = plan.extra[s, e]
                    act.wait_ge(t_done, base + n + 1)
                    if e == ("v", 0, 1, 2, 3):
                        act.wait_ge(v_out, 32 * (t + 1))                   
                    elif e == ("k", 4, 5, 6, 7):
                        act.wait_ge(k_out, 32 * (t + 1))
                    extra_act(act, e, 1 - par, (T_FIRST + n) % 2)
            if again:
                act.wait_ge(qkv_done, STEPS * (t + 1) + 9)
                Unit(t, par, 4).act(act)

        with act.Fori(0, PAIRS // 2 - 1) as j:
            pair(j, 0, True, True)
            pair(j, 1, True, True)
        pair(PAIRS // 2 - 1, 0, True, False)
        pair(PAIRS // 2 - 1, 1, False, False)
        ffn[0].split(act, None, 0, 0)
        for c in range(NCH):
            for d in range(KT):
                norm.act_tile(act, c, d)
        act.wait_ge(wo_done, 1 + BURST * PAIRS)

    def attention_dve(dve, norm):
        dve.wait_ge(rel_in, 16)
        dve.tensor_scalar(rel_rev[:, P:], rel_tab[:, 2 * P - 1::-1][:, :REV - P], rel_tab[:, 2 * P:], None,
                          ALU.subtract).then_inc(rel_done, 1)

        def qkv_out(u, c, bank, par):
            start, n = CH[c]
            src, r = psum[:, bank, :n], rstd[:, start:start + n]
            if u < 2:
                dst = chunk((stage, kT[par])[u], c)
                dve.tensor_tensor(dst, src, r, ALU.mult).then_inc(oq_free, 1)
                return
            cuts, at = [], start
            while at < start + n:
                if at == SEQ:
                    at = SMP
                end = start + n if at >= SMP else min(start + n, SEQ, (at // CK + 1) * CK)
                if at < SMP and at % CK == 0:
                    end = max(end, min(start + n, SEQ) // CK * CK)
                cuts.append((at, end))
                at = end
            for at, end in cuts:
                i, j = (SEQ // CK, 0) if at >= SMP else divmod(at, CK)
                m = end - at
                for h in range(2):
                    rows = slice(CK * h, CK * (h + 1))
                    a, b = src[rows, at - start:end - start], r[rows, at - start:end - start]
                    if m > CK:
                        dst = qd[par][rows, i:i + m // CK, CK * h:CK * (h + 1)]
                        a, b = (v.rearrange("p (c q) -> p c q", q=CK) for v in (a, b))
                    else:
                        dst = qd[par][rows, i, CK * h + j:CK * h + j + m]
                    last = dve.scalar_tensor_tensor(dst, a, SCALE, b, ALU.mult, ALU.mult)
            last.then_inc(oq_free, 1)

        for o in range(STEPS):
            u, c = divmod(o, NCH)
            if o == 2:
                norm_a.dve_row(dve, 2)
            if o == 6:
                dve.wait_ge(at_zero, 6)
                split_dve(dve, 3)
            dve.wait_ge(qkv_done, o + 1)
            qkv_out(u, c, 6 + o % 2, 0)
            if o == 2:
                split_dve(dve, 2)
        dve.wait_ge(bias_in, 32)

        def pair(half, par, following, again):
            t = 2 * half + par
            plan = PLAN[following]
            tiles = (2 * NB + 1) * t
            for s in range(STEPS + 1):
                if s:
                    bank = 6 + (OQ_FIRST + plan.o[s - 1]) % 2
                    dve.wait_ge(o_hi_done, 2 * STEPS * t + 2 * s)
                    for (dst, src), (hi, _) in zip(o_halves(s - 1, o_lo, bank), o_halves(s - 1, o_hi, bank)):
                        last = dve.tensor_tensor(dst, src, hi, ALU.subtract)
                    last.then_inc(oq_free, 1)
                if s == STEPS:
                    break
                for odd in chunks_of(s):
                    q = tiles + 2 * s + odd
                    first, n = chunk_scores(s, odd)
                    dve.wait_ge(qk_done, q + 1)
                    if s == NB:
                        part, b = psum[:, 0, PAST - P:n], bias[:, t, 0:P + DEC]
                    elif n > BANK:
                        part, b = psum[:, 2 * odd + 1, n // 2 - VAR:n // 2], bias[:, t, :]
                    else:
                        m = min(n, VAR)
                        part, b = psum[:, 2 * odd, n - m:n], bias[:, t, VAR - m:]
                    dve.tensor_tensor(part, part, b, ALU.add).then_inc(masked, 1)
                    dve.wait_ge(masked, q + 1)
                    dve.tensor_reduce(neg_max[:, odd:odd + 1], scores_of(s, odd), AX.XY if n > BANK else AX.X,
                                      ALU.max, negate=True).then_inc(max_done, 1)
                if s == 0:
                    Unit(t, par, 1 if following else 0).dve(dve)
                elif following and s in (3, 6):
                    Unit(t, par, s // 3 + 1).dve(dve)
                for odd in chunks_of(s):
                    q = tiles + 2 * s + odd
                    n = chunk_scores(s, odd)[1]
                    dve.wait_ge(exp_done, q + 1)
                    dve.reciprocal(row_inv[:, odd:odd + 1], row_sum[:, odd:odd + 1]).then_inc(inv_done, 1)
                    dve.wait_ge(inv_done, q + 1)
                    p = p_even[:, :n] if not odd else p_odd[:, CK:CK + n]
                    dve.tensor_scalar(p, p, row_inv[:, odd:odd + 1], None, ALU.mult).then_inc(p_done, 1)
                if following:
                    u, c = divmod(s, NCH)
                    dve.wait_ge(qkv_done, STEPS * (t + 1) + s + 1)
                    qkv_out(u, c, 6 + (OQ_FIRST + plan.q[s]) % 2, 1 - par)
            if again:
                Unit(t, par, 4).dve(dve)
            elif not following:
                ffn[0].split(None, dve, 0, 0)
            dve.wait_ge(at_added, BURST * t + 1)
            for n in range(BURST):
                c, d = divmod(n, KT)
                dve.wait_ge(wo_done, 1 + BURST * t + n + 1)
                dve.tensor_tensor(chunk(x[:, d, :], c), chunk(x[:, d, :], c), psum[:, n % 4, :CH[c][1]], ALU.add)\
                    .then_inc(at_added, 1)
                if not following and c:
                    norm.dve_tile(dve, c - 1, d)

        with dve.Fori(0, PAIRS // 2 - 1) as j:
            pair(j, 0, True, True)
            pair(j, 1, True, True)
        pair(PAIRS // 2 - 1, 0, True, False)
        pair(PAIRS // 2 - 1, 1, False, False)
        for d in range(KT):
            norm.dve_tile(dve, NCH - 1, d)

    DOWN = NCH * KT
    UP = 4 * NCH
    RING = 6
    WEIGHTS = 6

    class Ffn:

        gate_in = sem("ffn_gate_in")
        value_in = sem("ffn_value_in")
        down_in = sem("ffn_down_in")
        w_hi = sem("ffn_w_hi")
        w_lo = sem("ffn_w_lo")
        up = sem("ffn_up")
        down = sem("ffn_down")
        free = sem("ffn_free")
        added = sem("ffn_added")
        affine = sem("ffn_affine")
        conv1 = sem("ffn_conv1")
        conv = sem("ffn_conv")
        silu = sem("ffn_silu")
        prod = sem("ffn_prod")
        h_hi = sem("ffn_h_hi")
        h_lo = sem("ffn_h_lo")
        edge = sem("ffn_edge")
        cur = sem("ffn_cur")
        hist = sem("ffn_hist")
        tail = sem("ffn_tail")
        tails_turned = sem("ffn_tails_turned")
        tails_row = sem("ffn_tails_row")
        tails_out = sem("ffn_tails_out")

        def __init__(self, layer, norm_in, norm_out):
            self.layer, self.norm_in, self.norm_out = layer, norm_in, norm_out
            self.done = FIT * layer

        def up_src(self, value, it):
            return f_w_up[self.layer, :, bass.ds(FF * value + 2 * P * it, 2 * P)].rearrange("(k p) n -> p k n", p=P)

        def down_src(self, it):
            return f_w_down[self.layer, bass.ds(2 * P * it, 2 * P), :].rearrange("(i p) n -> p i n", p=P)

        def sp_first(self, sp):
            sp.dma_start(raw0[:, :].rearrange("p (k n) -> p k n", k=KT), self.up_src(0, 0)).then_inc(self.gate_in, 16)

        def sp(self, sp, region_free, next_load):
            region_free(sp)
            sp.dma_start(raw1[:, :].rearrange("p (k n) -> p k n", k=KT), self.up_src(1, 0)).then_inc(self.value_in, 16)

            def iteration(it, last):
                done = self.done + it
                sp.wait_ge(self.w_lo, WEIGHTS * done + 3)
                stand(sp)
                sp.dma_start(raw0[:, :].rearrange("p (i n) -> p i n", i=2), self.down_src(it)).then_inc(self.down_in, 16)
                if not last:
                    sp.wait_ge(self.w_lo, WEIGHTS * done + 4)
                    stand(sp)
                    sp.dma_start(raw1[:, :].rearrange("p (k n) -> p k n", k=KT), self.up_src(1, it + 1))\
                        .then_inc(self.value_in, 16)
                    sp.wait_ge(self.w_lo, WEIGHTS * done + 6)
                    stand(sp)
                    sp.dma_start(raw0[:, :].rearrange("p (k n) -> p k n", k=KT), self.up_src(0, it + 1))\
                        .then_inc(self.gate_in, 16)

            iteration(0, False)
            with sp.Fori(1, FIT - 1) as it:
                iteration(it, False)
            iteration(FIT - 1, True)
            next_load(sp)
            sp.wait_ge(self.tails_row, 2 * self.layer + 2)
            for i, dst in enumerate((new_conv_prompt, new_conv_sample)):
                sp.dma_start(dst[self.layer, 0].rearrange("j (t p) -> (j t) p", p=P), tails_row[:2 * CT, i, :])\
                    .then_inc(self.tails_out, 16)

        def raw_of(self, u):
            if u >= 4:
                return raw0[:, 1024 * (u - 4):1024 * (u - 3)]
            both = (raw0, raw1)[u % 2][:, :].rearrange("p (k i n) -> p k i n", k=KT, i=2)
            return both[:, :, u // 2, :]

        def slot_of(self, u):
            return u % 2 if u < 4 else u - 2

        def split(self, act, dve, it, u):
            slot, done = self.slot_of(u), self.done + it
            count = WEIGHTS * done + u + 1
            shape = (lambda w: w[:, :]) if u >= 4 else (lambda w: w[:, :].rearrange("p (k n) -> p k n", k=KT))
            if act is not None:
                act.wait_ge((self.gate_in, self.value_in, self.gate_in, self.value_in, self.down_in, self.down_in)[u],
                            16 * (done + 1))
                if u >= 4:
                    pass
                elif u >= 2:
                    act.wait_ge(self.up, UP * done + NCH * (u - 1))
                else:
                    at_least(act, self.up, UP * done - UP + NCH * (u + 3))
                act.activation(shape(f_hi[slot]), self.raw_of(u), ACT.Copy).then_inc(self.w_hi, 1)
            else:
                dve.wait_ge(self.w_hi, count)
                dve.tensor_tensor(shape(f_lo[slot]), self.raw_of(u), shape(f_hi[slot]), ALU.subtract)\
                    .then_inc(self.w_lo, 1)

        SPLITS = {3: 2, 6: 3, 7: 4, 8: 5}
        NEXT_SPLITS = {2: 0, 7: 1}

        def pe(self, pe, banks_free):
            ring = RING

            def iteration(it, first, last):
                done = self.done + it
                for o in range(UP):
                    u, c = divmod(o, NCH)
                    if first and u == 0:
                        self.norm_in.pe_sum(pe, c)
                        pe.wait_ge(Norm.lo, self.norm_in.tiles + KT * (c + 1))
                    if c == 0:
                        pe.wait_ge(self.w_lo, WEIGHTS * done + u + 1)
                    if o >= RING:
                        pe.wait_ge(self.free, RING + UP * done + o - RING + 1)
                    elif first:
                        banks_free(pe)
                    else:
                        pe.wait_ge(self.added, DOWN * done - RING + o + 1)
                    linear(pe, psum[:, o % ring, :CH[c][1]], f_hi[u % 2], f_lo[u % 2], c).then_inc(self.up, 1)
                for n in range(DOWN):
                    c, d = divmod(n, KT)
                    if n == 0:
                        pe.wait_ge(self.w_lo, WEIGHTS * done + 6)
                    if d == 0:
                        pe.wait_ge(self.h_lo, 2 * NCH * done + NCH + c + 1)
                    if n >= RING:
                        pe.wait_ge(self.added, DOWN * done + n - RING + 1)
                    else:
                        pe.wait_ge(self.free, RING + UP * (done + 1) - RING + n + 1)
                    cut = slice(P * d, P * (d + 1))
                    for i in range(2):
                        mm = product(pe, psum[:, n % ring, :CH[c][1]], (f_hi[2 + i][:, cut], f_lo[2 + i][:, cut]),
                                     (chunk(h_hi[i][:, :], c), chunk(h_lo[i][:, :], c)), i == 0, i == 1)
                    mm.then_inc(self.down, 1)

            iteration(0, True, False)
            with pe.Fori(1, FIT - 1) as it:
                iteration(it, False, False)
            iteration(FIT - 1, False, True)
            pe.wait_ge(self.tail, 2 * 4 * (self.done + FIT))
            for i in range(2):
                pe.transpose(psum[:2 * CT, 6, P * i:P * (i + 1)], tails[:, 2 * i:2 * i + 2, :].rearrange("p j t -> p (j t)"),
                             ident[:, :]).then_inc(self.tails_turned, 1)

        def pieces(self, c):
            start, n = CH[c]
            return [(start, start + n)] if c < NCH - 1 else [(start, SEQ), (SMP, TW)]

        def act(self, act, next_split):
            self.split(act, None, 0, 1)

            def value_hi(done, o):
                i, c = o // (2 * NCH), o % NCH
                start, n = CH[c]
                act.wait_ge(self.prod, 2 * NCH * done + NCH * i + c + 1)
                act.activation(h_hi[i][:, start:start + n], prod[:, k_par(c, i), :n], ACT.Copy).then_inc(self.h_hi, 1)

            def iteration(it, first, last):
                done = self.done + it
                for o in range(UP):
                    u, c = divmod(o, NCH)
                    g, i = u % 2, u // 2
                    start, n = CH[c]
                    if o in self.SPLITS:
                        self.split(act, None, it, self.SPLITS[o])
                    if o and (o - 1) // NCH % 2:
                        value_hi(done, o - 1)
                    if first and u == 0:
                        self.norm_in.act_root(act, c)
                    act.wait_ge(self.free, RING + UP * done + o + 1)
                    if c == 0:
                        act.wait_ge(self.cur, 2 * done + 2)
                    if c == NCH - 1:
                        act.wait_ge(self.hist, 4 * done + u + 1)
                    po = o - 2
                    if po >= 0 or not first:
                        pu = (po % UP) // NCH
                        if pu % 2:
                            before = 2 * NCH * done + (po % UP) // (2 * NCH) * NCH + po % NCH + 1
                            act.wait_ge(self.prod, before if po >= 0 else before - 2 * NCH)
                        else:
                            before = 2 * NCH * done + (po % UP) // (2 * NCH) * NCH + po % NCH + 1
                            act.wait_ge(self.silu, before)
                    act.activation(conv_t[:, o % 2, :n], a_buf[g][:, start + 2:start + 2 + n], ACT.Identity,
                                   scale=cur[:, 2, g, i:i + 1], bias=cur[:, 3, g, i:i + 1]).then_inc(self.affine, 1)
                    k = 2 * NCH * done + NCH * i + c
                    if g == 0:
                        act.wait_ge(self.conv, UP * done + o + 1)
                        act.activation(s_gate[:, start:start + n], conv_t[:, o % 2, :n], ACT.Silu).then_inc(self.silu, 1)
                value_hi(done, UP - 1)
                for n in range(DOWN):
                    c, d = divmod(n, KT)
                    if n in self.NEXT_SPLITS:
                        if not last:
                            self.split(act, None, it + 1, self.NEXT_SPLITS[n])
                        elif self.NEXT_SPLITS[n] == 0:
                            next_split(act, None)
                    if last:
                        self.norm_out.act_tile(act, c, d)

            iteration(0, True, False)
            with act.Fori(1, FIT - 1) as it:
                iteration(it, False, False)
            iteration(FIT - 1, False, True)
            for i in range(2):
                act.wait_ge(self.tails_turned, 2 * self.layer + 2)
                act.activation(tails_row[:2 * CT, i, :], psum[:2 * CT, 6, P * i:P * (i + 1)], ACT.Copy)\
                    .then_inc(self.tails_row, 1)

        def dve(self, dve, next_split):
            self.split(None, dve, 0, 1)

            def value_lo(done, o):
                i, c = o // (2 * NCH), o % NCH
                start, n = CH[c]
                dve.wait_ge(self.h_hi, 2 * NCH * done + NCH * i + c + 1)
                dve.tensor_tensor(h_lo[i][:, start:start + n], prod[:, k_par(c, i), :n], h_hi[i][:, start:start + n],
                                  ALU.subtract).then_inc(self.h_lo, 1)

            def iteration(it, first, last):
                done = self.done + it
                for o in range(UP):
                    u, c = divmod(o, NCH)
                    g, i = u % 2, u // 2
                    start, n = CH[c]
                    if first and u == 0:
                        self.norm_in.dve_row(dve, c)
                    dve.wait_ge(self.up, UP * done + o + 1)
                    if first and o in (0, NCH):
                        dve.wait_ge(self.edge, 2 * self.layer + 2)
                    for a, b in self.pieces(c):
                        mm = dve.tensor_tensor(a_buf[g][:, a + 2:b + 2], psum[:, o % RING, a - start:b - start],
                                               rstd[:, a:b], ALU.mult)
                    mm.then_inc(self.free, 1)
                    if o and (o - 1) // NCH % 2:
                        value_lo(done, o - 1)
                    t = conv_t[:, o % 2, :n]
                    dve.wait_ge(self.affine, UP * done + o + 1)
                    dve.scalar_tensor_tensor(t, a_buf[g][:, start + 1:start + 1 + n], cur[:, 1, g, i:i + 1], t,
                                             ALU.mult, ALU.add).then_inc(self.conv1, 1)
                    dve.wait_ge(self.conv1, UP * done + o + 1)
                    dve.scalar_tensor_tensor(t, a_buf[g][:, start:start + n], cur[:, 0, g, i:i + 1], t,
                                             ALU.mult, ALU.add).then_inc(self.conv, 1)
                    if g == 1:
                        k = 2 * NCH * done + NCH * i + c
                        dve.wait_ge(self.conv, UP * done + o + 1)
                        dve.wait_ge(self.silu, k + 1)
                        pr = prod[:, k_par(c, i), :n]
                        dve.tensor_tensor(pr, t, s_gate[:, start:start + n], ALU.mult).then_inc(self.prod, 1)
                    if o in self.SPLITS:
                        self.split(None, dve, it, self.SPLITS[o])
                value_lo(done, UP - 1)
                at_least(dve, self.added, DOWN * done)
                for n in range(DOWN):
                    c, d = divmod(n, KT)
                    if n in self.NEXT_SPLITS:
                        if not last:
                            self.split(None, dve, it + 1, self.NEXT_SPLITS[n])
                        elif self.NEXT_SPLITS[n] == 0:
                            next_split(None, dve)
                    dve.wait_ge(self.down, DOWN * done + n + 1)
                    mm = dve.tensor_tensor(chunk(x[:, d, :], c), chunk(x[:, d, :], c), psum[:, n % RING, :CH[c][1]],
                                           ALU.add)
                    mm.then_inc(self.added, 1)
                    if last and c:
                        self.norm_out.dve_tile(dve, c - 1, d)

            iteration(0, True, False)
            with dve.Fori(1, FIT - 1) as it:
                iteration(it, False, False)
            iteration(FIT - 1, False, True)
            for d in range(KT):
                self.norm_out.dve_tile(dve, NCH - 1, d)

        def pool(self, pool, region_free):
            for c in range(NCH - 1):
                self.norm_in.pool(pool, c)
            region_free(pool)
            for t in (a_gate, a_val):
                pool.memset(t[:, 0:2], 0.0).then_inc(self.edge, 1)

            def iteration(it, first, last):
                done = self.done + it
                at_least(pool, self.conv, UP * done)
                stand(pool)
                for g in range(2):
                    pool.tensor_copy(cur[:, :, g, :], taps[self.layer][:, :, bass.ds(FT * g + 2 * it, 2)])\
                        .then_inc(self.cur, 1)
                if first:
                    self.norm_in.pool(pool, NCH - 1)
                pool.wait_ge(self.cur, 2 * done + 2)
                stand(pool)
                for u in range(4):
                    g, i = u % 2, u // 2
                    if u >= 2:
                        pool.wait_ge(self.conv, UP * done + NCH * (u - 1))
                        stand(pool)
                    pool.tensor_copy(a_buf[g][:, SMP:SMP + 2], cur[:, 4:6, g, i]).then_inc(self.hist, 1)
                    pool.wait_ge(self.free, RING + UP * done + NCH * (u + 1))
                    stand(pool)
                    for r, col in enumerate((SEQ, TW)):
                        pool.tensor_copy(tails[:, 2 * r:2 * r + 2, bass.ds(FT * g + 2 * it + i, 1)],
                                         a_buf[g][:, col:col + 2].rearrange("p (j o) -> p j o", o=1))\
                            .then_inc(self.tail, 1)

            iteration(0, True, False)
            with pool.Fori(1, FIT - 1) as it:
                iteration(it, False, False)
            iteration(FIT - 1, False, True)

    def k_par(c, i):
        return (NCH * i + c) % 2

    SETS = KT // 2
    OUT6 = 2 * NCH
    g_raw = sem("g_raw")
    g_hi = sem("g_hi")
    g_lo = sem("g_lo")
    g_out = sem("g_out")
    g_free = sem("g_free")
    gelu_done = sem("gelu_done")
    v_squared = sem("v_squared")
    v_added = sem("v_added")
    ws_in = sem("ws_in")
    bs_in = sem("bs_in")
    ws_turned = sem("ws_turned")
    ws_copied = sem("ws_copied")
    g_zero = sem("g_zero")
    v_sum = sem("v_sum")
    v_mean = sem("v_mean")
    v_root = sem("v_root")
    v_rstd = sem("v_rstd")
    vt_turned = sem("vt_turned")
    vt_copied = sem("vt_copied")
    mix_done = sem("mix_done")
    mix_added = sem("mix_added")
    gated = sem("gated")
    gs_hi = sem("gs_hi")
    gs_lo = sem("gs_lo")
    g_added = sem("g_added")
    gv_out = sem("gv_out")
    HALF = CK

    def raw_unit(u):
        return raw0[:, :].rearrange("p (k i n) -> p k i n", k=KT, i=2)[:, :, u, :]

    def g_split(act, dve, i, u):
        if act is not None:
            act.wait_ge(g_raw, 16 * (i + 1))
            act.activation(w_hi[u][:, :].rearrange("p (k n) -> p k n", k=KT), raw_unit(u), ACT.Copy).then_inc(g_hi, 1)
        else:
            dve.wait_ge(g_hi, 2 * i + u + 1)
            dve.tensor_tensor(w_lo[u][:, :].rearrange("p (k n) -> p k n", k=KT), raw_unit(u),
                              w_hi[u][:, :].rearrange("p (k n) -> p k n", k=KT), ALU.subtract).then_inc(g_lo, 1)

    def g_splits(act, dve, i, o, last=False):
        if o == 1:
            if act is not None:
                at_least(act, g_out, OUT6 * i)
            g_split(act, dve, i, 1)
        if o == 5 and not last:
            if act is not None:
                act.wait_ge(g_out, OUT6 * i + NCH)
            g_split(act, dve, i + 1, 0)

    def g_sp(sp, region_free):
        def load(src):
            sp.dma_start(raw0[:, :].rearrange("p (k n) -> p k n", k=KT), src.rearrange("(k p) n -> p k n", p=P))\
                .then_inc(g_raw, 16)

        region_free(sp)
        sp.dma_start(vt0[:, :, :, :].rearrange("p k h n -> p (k h) n"), b_w_s[0].rearrange("g p q -> p g q"))\
            .then_inc(ws_in, 16)
        for h in range(2):
            src = bass.AP(b_bias_s.tensor, h * P, [[0, HALF], [2 * P, KT], [1, P]])
            sp.dma_start(bs[HALF * h:HALF * (h + 1), :, :], src).then_inc(bs_in, 16)
        sp.dma_start(gain_v[:, :], bass.AP(b_v_norm.tensor, 0, [[0, P], [1, D]])).then_inc(bs_in, 16)
        for i in range(1, SETS):
            sp.wait_ge(g_lo, 2 * i)
            load(b_w_in[0, :, D + 2 * P * i:D + 2 * P * (i + 1)])
        with sp.Fori(SETS, 2 * SETS) as i:
            sp.wait_ge(g_lo, 2 * i)
            stand(sp)
            load(b_w_in[0, :, bass.ds(2 * P * (i - SETS), 2 * P)])
        sp.wait_ge(vt_copied, NB + 1)
        for h in range(2):
            sp.dma_start(new_gmlp_v[0, 0].rearrange("t (k h e) -> t k h e", h=2, e=HALF)[:, :, h, :],
                         v_pad[NB % 2][:DEC, :, h, HALF * h:HALF * (h + 1)]).then_inc(gv_out, 16)
        with sp.Fori(2 * SETS, 3 * SETS) as i:
            sp.wait_ge(g_lo, 2 * i)
            stand(sp)
            load(b_w_out[0, :, bass.ds(2 * P * (i - 2 * SETS), 2 * P)])

    def g_sp_first(sp):
        sp.wait_ge(ffn[0].w_lo, WEIGHTS * FIT)
        sp.dma_start(raw0[:, :].rearrange("p (k n) -> p k n", k=KT),
                     b_w_in[0, :, D:D + 2 * P].rearrange("(k p) n -> p k n", p=P)).then_inc(g_raw, 16)

    def mixing(turn, mix):
        for b in range(NB + 3):
            if b < NB + 1:
                turn(b)
            if b >= 2:
                mix(b - 2)

    def g_pe(pe, norm):
        def outputs(i, wait):
            for o in range(OUT6):
                u, c = divmod(o, NCH)
                wait(o, u, c)
                if c == 0:
                    pe.wait_ge(g_lo, 2 * i + u + 1)
                pe.wait_ge(g_free, OUT6 * i + o + 1)
                linear(pe, psum[:, o, :CH[c][1]], w_hi[u], w_lo[u], c).then_inc(g_out, 1)

        def first(o, u, c):
            if o == 0:
                pe.wait_ge(Ffn.added, DOWN * FIT)
            if u == 0:
                norm.pe_sum(pe, c)
                pe.wait_ge(Norm.lo, norm.tiles + KT * (c + 1))

        outputs(0, first)
        pe.wait_ge(ws_in, 16)
        pe.wait_ge(Norm.mean, norm.chunks + NCH)
        for j in range(GROUPS // 4):
            at_least(pe, ws_copied, j - 1)
            for k in range(4):
                g = 4 * j + k
                mm = pe.transpose(psum[:, 6 + j % 2, P * k:P * (k + 1)], vt0[:, g // 2, g % 2, :], ident[:, :])
            mm.then_inc(ws_turned, 1)
        with pe.Fori(1, SETS) as i:
            outputs(i, lambda o, u, c: None)
        pe.wait_ge(v_added, NCH * KT)
        for b, (start, n) in enumerate(BLOCKS):
            mm = pe.matmul(psum[:n, 7, 2 * b:2 * b + 2], total[:, start:start + n], ones[:, 0:2], start=True, stop=True)
        mm.then_inc(v_sum, 1)
        pe.wait_ge(g_free, RING + OUT6 * SETS)
        pe.wait_ge(gelu_done, OUT6 * SETS)

        def turn(b):
            start, n = BLOCKS[b]
            at_least(pe, vt_copied, b - 1)
            for d in range(KT):
                mm = pe.transpose(psum[:n, 2 * (b % 2) + d // 4, P * (d % 4):P * (d % 4 + 1)],
                                  vT[:, d, start:start + n], ident[:, :])
            mm.then_inc(vt_turned, 1)

        def mix(b):
            n = BLOCKS[b][1]
            if b == 0:
                pe.wait_ge(g_zero, 3)
            pe.wait_ge(vt_copied, b + 1)
            at_least(pe, mix_added, b - 1)
            for d in range(KT):
                for h in range(2):
                    mm = pe.matmul(psum[:, 4 + 2 * (b % 2) + d // 4, P * (d % 4):P * (d % 4) + n],
                                   v_pad[b % 2][:n, d, h, :], wsT[:n, 2 * d + h, :n], start=(h == 0), stop=(h == 1))
            mm.then_inc(mix_done, 1)

        mixing(turn, mix)
        pe.wait_ge(mix_added, NB + 1)
        with pe.Fori(SETS, 2 * SETS) as i:
            outputs(i, lambda o, u, c: None)
        with pe.Fori(2 * SETS, 3 * SETS) as i:
            outputs(i, lambda o, u, c: pe.wait_ge(gs_lo, KT * (c + 1)))

    def g_act(act, norm, norm_out):
        def v_set(i, first):
            for o in range(OUT6):
                u, c = divmod(o, NCH)
                n = CH[c][1]
                if first and u == 0:
                    norm.act_root(act, c)
                g_splits(act, None, i, o)
                act.wait_ge(g_free, RING + OUT6 * i + o + 1)
                if not first:
                    stand(act)
                dst = chunk(vT, c)[:, 2 * i + u, :] if isinstance(i, int) else chunk(vT, c)[:, bass.ds(2 * i + u, 1), :]
                src = gm_t[:, o % 2, :n] if isinstance(i, int) else gm_t[:, o % 2:o % 2 + 1, :n]
                act.activation(dst, src, ACT.Gelu).then_inc(gelu_done, 1)
                if first and o < 2:
                    act.wait_ge(Norm.added, norm.tiles + NCH * KT)
                else:
                    act.wait_ge(v_added, OUT6 * i + o - 1)
                act.wait_ge(gelu_done, OUT6 * i + o + 1)
                if not first:
                    stand(act)
                sq = squares[:, o % 2, :n] if isinstance(i, int) else squares[:, o % 2:o % 2 + 1, :n]
                act.activation(sq, dst, ACT.Square).then_inc(v_squared, 1)

        v_set(0, True)
        for j in range(GROUPS // 4):
            act.wait_ge(ws_turned, j + 1)
            act.activation(wsT[:, 4 * j:4 * j + 4, :].rearrange("p g n -> p (g n)"), psum[:, 6 + j % 2, :],
                           ACT.Copy).then_inc(ws_copied, 1)
        with act.Fori(1, SETS) as i:
            v_set(i, False)
        act.wait_ge(v_mean, 2)
        act.activation(rc_v[:, :NB], rc_v[:, :NB], ACT.Sqrt).then_inc(v_root, 1)
        act.activation(rc_v[:DEC, NB:], rc_v[:DEC, NB:], ACT.Sqrt).then_inc(v_root, 1)
        with act.Fori(SETS, 2 * SETS) as i:
            for o in range(OUT6):
                n = CH[o % NCH][1]
                g_splits(act, None, i, o)
                act.wait_ge(g_free, RING + OUT6 * i + o + 1)
                act.activation(gm_t[:, o % 2, :n], gm_t[:, o % 2, :n], ACT.Gelu).then_inc(gelu_done, 1)
        act.wait_ge(gated, 2 + NCH * KT)
        for c in range(NCH):
            for d in range(KT):
                act.activation(chunk(gx_hi[:, d, :], c), chunk(vT[:, d, :], c), ACT.Copy).then_inc(gs_hi, 1)

        def w_out_set(i, last):
            for o in range(OUT6):
                g_splits(act, None, i, o, last)
                if last and o == 5:
                    act.wait_ge(g_out, OUT6 * i + NCH)
                    ffn[1].split(act, None, 0, 0)

        with act.Fori(2 * SETS, 3 * SETS - 1) as i:
            w_out_set(i, False)
        w_out_set(3 * SETS - 1, True)
        for c in range(NCH):
            for d in range(KT):
                norm_out.act_tile(act, c, d)

    def g_dve(dve, norm, norm_out):
        def to_buffer(i, o):
            start, n = CH[o % NCH]
            dve.wait_ge(g_out, OUT6 * i + o + 1)
            dve.tensor_tensor(gm_t[:, o % 2, :n], psum[:, o, :n], rstd[:, start:start + n], ALU.mult).then_inc(g_free, 1)

        def v_set(i, first):
            for o in range(OUT6):
                if first and o < NCH:
                    norm.dve_row(dve, o)
                g_splits(None, dve, i, o)
                if not first or o >= 2:
                    dve.wait_ge(gelu_done, OUT6 * i + o - 1)
                elif o == 0:
                    dve.wait_ge(ws_in, 16)
                to_buffer(i, o)

        v_set(0, True)
        with dve.Fori(1, SETS) as i:
            v_set(i, False)
        dve.wait_ge(v_sum, 1)
        sums = psum[:, 7, :2 * (NB + 1)].rearrange("p (b i) -> p b i", i=2)
        for rows, cut in ((slice(0, P), slice(0, NB)), (slice(0, DEC), slice(NB, NB + 1))):
            dve.tensor_scalar(rc_v[rows, cut], sums[rows, cut, 0], 1.0 / D, EPS, ALU.mult, ALU.add).then_inc(v_mean, 1)
        for k, (rows, cut) in enumerate(((slice(0, P), slice(0, NB)), (slice(0, DEC), slice(NB, NB + 1)))):
            dve.wait_ge(v_root, k + 1)
            dve.reciprocal(rc_v[rows, cut], rc_v[rows, cut]).then_inc(v_rstd, 1)
        dve.wait_ge(v_rstd, 2)
        dve.wait_ge(bs_in, 48)
        dve.wait_ge(g_zero, 2)

        def turn(b):
            n = BLOCKS[b][1]
            dve.wait_ge(vt_turned, b + 1)
            at_least(dve, mix_done, b - 1)
            for bank in range(2):
                src = psum[:n, 2 * (b % 2) + bank, :].rearrange("p (k h e) -> p k h e", h=2, e=HALF)
                g = gain_v[:n, :].rearrange("p (k h e) -> p k h e", h=2, e=HALF)[:, 4 * bank:4 * bank + 4]
                for h in range(2):
                    mm = dve.scalar_tensor_tensor(v_pad[b % 2][:n, 4 * bank:4 * bank + 4, h, HALF * h:HALF * (h + 1)],
                                                  src[:, :, h, :], rc_v[:n, b:b + 1], g[:, :, h, :], ALU.mult, ALU.mult)
            mm.then_inc(vt_copied, 1)

        def mix(b):
            start, n = BLOCKS[b]
            dve.wait_ge(mix_done, b + 1)
            for bank in range(2):
                src = psum[:, 4 + 2 * (b % 2) + bank, :].rearrange("p (k n) -> p k n", n=P)[:, :, :n]
                mm = dve.tensor_tensor(vT[:, 4 * bank:4 * bank + 4, start:start + n], src,
                                       bs[:, 4 * bank:4 * bank + 4, :n], ALU.add)
            mm.then_inc(mix_added, 1)

        mixing(turn, mix)
        with dve.Fori(SETS, 2 * SETS) as i:
            for o in range(OUT6):
                g_splits(None, dve, i, o)
                dve.wait_ge(gated, OUT6 * (i - SETS) + o + 1)
                to_buffer(i, o)
        for c in range(NCH):
            for d in range(KT):
                dve.wait_ge(gs_hi, KT * c + d + 1)
                dve.tensor_tensor(chunk(gx_lo[:, d, :], c), chunk(vT[:, d, :], c), chunk(gx_hi[:, d, :], c),
                                  ALU.subtract).then_inc(gs_lo, 1)

        def w_out_set(i, last):
            for o in range(OUT6):
                u, c = divmod(o, NCH)
                g_splits(None, dve, i, o, last)
                if last and o == 5:
                    ffn[1].split(None, dve, 0, 0)
                dve.wait_ge(g_out, OUT6 * i + o + 1)
                tile = chunk(x, c)[:, bass.ds(2 * (i - 2 * SETS) + u, 1), :]
                mm = dve.tensor_tensor(tile, tile, psum[:, o:o + 1, :CH[c][1]], ALU.add)
                mm.then_inc(g_free, 1)

        with dve.Fori(2 * SETS, 3 * SETS - 1) as i:
            w_out_set(i, False)
        w_out_set(3 * SETS - 1, True)
        for c in range(NCH):
            for d in range(KT):
                norm_out.dve_tile(dve, c, d)

    def g_pool(pool, norm, region_free):
        for c in range(NCH):
            norm.pool(pool, c)

        def sums(i, first):
            for o in range(OUT6):
                u, c = divmod(o, NCH)
                k = OUT6 * i + o
                sq = squares[:, o % 2, :CH[c][1]]
                pool.wait_ge(v_squared, k + 1)
                if first and u == 0:
                    pool.wait_ge(Norm.summed, norm.chunks + c + 1)
                    pool.tensor_copy(chunk(total, c), sq).then_inc(v_added, 1)
                else:
                    pool.wait_ge(v_added, k - NCH + 1)
                    pool.tensor_tensor(chunk(total, c), chunk(total, c), sq, ALU.add).then_inc(v_added, 1)

        sums(0, True)
        pool.wait_ge(ws_in, 16)
        pool.memset(vt1[:, :, :, :], 0.0).then_inc(g_zero, 1)
        pool.wait_ge(ws_copied, GROUPS // 4)
        pool.memset(vt0[:, :, :, :], 0.0).then_inc(g_zero, 1)
        pool.wait_ge(g_zero, 2)
        pool.memset(wsT[CK:, :, :CK], 0.0).then_inc(g_zero, 1)
        pool.wait_ge(g_zero, 3)
        with pool.Fori(1, SETS) as i:
            sums(i, False)
        pool.sem_inc(gated, 2)
        pool.wait_ge(mix_added, NB + 1)
        with pool.Fori(SETS, 2 * SETS) as i:
            for o in range(OUT6):
                u, c = divmod(o, NCH)
                pool.wait_ge(gelu_done, OUT6 * i + o + 1)
                tile = chunk(vT, c)[:, bass.ds(2 * (i - SETS) + u, 1), :]
                pool.tensor_tensor(tile, tile, gm_t[:, o % 2:o % 2 + 1, :CH[c][1]], ALU.mult).then_inc(gated, 1)

    fg_in = sem("fg_in")
    y_sum = sem("y_sum")
    y_mean = sem("y_mean")
    y_root = sem("y_root")
    y_rstd = sem("y_rstd")
    y_turned = sem("y_turned")
    y_done = sem("y_done")
    y_out = [sem(f"y_out{i}") for i in range(2)]

    def final_pe(pe, norm):
        pe.wait_ge(Norm.added, norm.tiles + NCH * KT)
        for b, (start, n) in enumerate(BLOCKS):
            mm = pe.matmul(psum[:n, 7, 2 * b:2 * b + 2], total[:, start:start + n], ones[:, 0:2], start=True, stop=True)
        mm.then_inc(y_sum, 1)
        pe.wait_ge(Ffn.added, DEPTH * DOWN * FIT)
        for b, (start, n) in enumerate(BLOCKS):
            at_least(pe, y_done, b - 2)
            for d in range(KT):
                mm = pe.transpose(psum[:n, 2 * (b % 3) + d // 4, P * (d % 4):P * (d % 4 + 1)],
                                  x[:, d, start:start + n], ident[:, :])
            mm.then_inc(y_turned, 1)

    def final_act(act):
        act.wait_ge(y_mean, 2)
        act.activation(rcol[:, :NB], rcol[:, :NB], ACT.Sqrt).then_inc(y_root, 1)
        act.activation(rcol[:DEC, NB:], rcol[:DEC, NB:], ACT.Sqrt).then_inc(y_root, 1)

    def final_dve(dve):
        dve.wait_ge(y_sum, 1)
        sums = psum[:, 7, :2 * (NB + 1)].rearrange("p (b i) -> p b i", i=2)
        parts = ((slice(0, P), slice(0, NB)), (slice(0, DEC), slice(NB, NB + 1)))
        for rows, cut in parts:
            dve.tensor_scalar(rcol[rows, cut], sums[rows, cut, 0], 1.0 / D, EPS, ALU.mult, ALU.add).then_inc(y_mean, 1)
        for k, (rows, cut) in enumerate(parts):
            dve.wait_ge(y_root, k + 1)
            dve.reciprocal(rcol[rows, cut], rcol[rows, cut]).then_inc(y_rstd, 1)
        dve.wait_ge(y_rstd, 2)
        dve.wait_ge(fg_in, 16)
        for b, (start, n) in enumerate(BLOCKS):
            dve.wait_ge(y_turned, b + 1)
            at_least(dve, y_out[b % 2], 16 * (b // 2))
            for i in range(2):
                cut = slice(BANK * i, BANK * (i + 1))
                mm = dve.scalar_tensor_tensor(y_tile[b % 2][:n, cut], psum[:n, 2 * (b % 3) + i, :], rcol[:n, b:b + 1],
                                              final_g[:n, cut], ALU.mult, ALU.mult)
            mm.then_inc(y_done, 1)

    def final_sp_first(sp):
        sp.wait_ge(ffn[1].w_lo, WEIGHTS * (2 * FIT - 1) + 4)
        sp.dma_start(final_g[:, :], bass.AP(ln_final.tensor, 0, [[0, P], [1, D]])).then_inc(fg_in, 16)

    def final_sp(sp):
        for b, (start, n) in enumerate(BLOCKS):
            sp.wait_ge(y_done, b + 1)
            dst = y_prompt[0, start:start + n, :] if b < NB else y_sample[0]
            sp.dma_start(dst, y_tile[b % 2][:n, :]).then_inc(y_out[b % 2], 16)

    def attention_over(engine):
        engine.wait_ge(at_added, 1 + BURST * PAIRS)
        engine.wait_ge(k_out, 32 * PAIRS)
        engine.wait_ge(v_out, 32 * PAIRS)

    def ffn0_over(engine):
        engine.wait_ge(ffn[0].added, DOWN * FIT)
        engine.wait_ge(ffn[0].tails_out, 32)

    def gmlp_over(engine):
        engine.wait_ge(g_free, RING + 3 * SETS * OUT6)
        engine.wait_ge(gs_lo, NCH * KT)
        engine.wait_ge(gv_out, 32)

    ffn = []
    norm_b = Norm(1, 2, lambda e, c, d: e.wait_ge(at_added, 1 + BURST * (PAIRS - 1) + KT * c + d + 1))
    norm_c = Norm(2, 1, lambda e, c, d: e.wait_ge(ffn[0].added, DOWN * (FIT - 1) + KT * c + d + 1))
    norm_d = Norm(3, 3, lambda e, c, d: e.wait_ge(g_free, RING + 3 * SETS * OUT6))
    norm_e = Norm(4, 4, lambda e, c, d: e.wait_ge(ffn[1].added, DOWN * (2 * FIT - 1) + KT * c + d + 1), split=False)
    ffn.append(Ffn(0, norm_b, norm_c))
    ffn.append(Ffn(1, norm_d, norm_e))

    block = ctx.enter_context(nc.Block())

    @block.sync
    def _(sp):
        attention_first_sp(sp)
        input_sp(sp)
        attention_second_sp(sp)
        attention_sp(sp)
        sp.wait_ge(at_lo, 4 * PAIRS)
        ffn[0].sp_first(sp)
        ffn[0].sp(sp, attention_over, g_sp_first)
        g_sp(sp, ffn0_over)
        sp.wait_ge(g_lo, 2 * 3 * SETS)
        ffn[1].sp_first(sp)
        ffn[1].sp(sp, gmlp_over, final_sp_first)
        final_sp(sp)
        for semaphore, stores in ((k_out, 2 * PAIRS), (v_out, 2 * PAIRS), (gv_out, 2), (Ffn.tails_out, 2 * DEPTH),
                                  (y_out[0], NB // 2 + 1), (y_out[1], NB // 2)):
            sp.wait_ge(semaphore, 16 * stores)

    @block.gpsimd
    def _(pool):
        input_pool(pool)
        for c in range(NCH):
            norm_a.pool(pool, c)
        attention_pool(pool)
        ffn[0].pool(pool, attention_over)
        g_pool(pool, norm_c, ffn0_over)
        ffn[1].pool(pool, gmlp_over)
        for c in range(NCH):
            norm_e.pool(pool, c)

    @block.scalar
    def _(act):
        act.sem_inc(t_free, 2)
        input_act_dma(act)
        input_act(act)
        attention_act(act, norm_b)
        ffn[0].act(act, lambda a, d: g_split(a, d, 0, 0))
        g_act(act, norm_c, norm_d)
        act.wait_ge(g_out, OUT6 * 3 * SETS)
        ffn[1].act(act, lambda a, d: None)
        final_act(act)

    @block.tensor
    def _(pe):
        pe.sem_inc(pv_done, 1)
        pe.sem_inc(wo_done, 1)
        input_pe(pe)
        attention_pe(pe)
        ffn[0].pe(pe, lambda e: e.wait_ge(at_added, 1 + BURST * PAIRS))
        g_pe(pe, norm_c)
        ffn[1].pe(pe, lambda e: e.wait_ge(g_free, RING + 3 * SETS * OUT6))
        final_pe(pe, norm_e)

    @block.vector
    def _(dve):
        dve.sem_inc(oq_free, 2)
        dve.sem_inc(at_added, 1)
        dve.sem_inc(Ffn.free, RING)
        dve.sem_inc(g_free, RING)
        input_dve(dve)
        attention_dve(dve, norm_b)
        ffn[0].dve(dve, lambda a, d: g_split(a, d, 0, 0))
        g_dve(dve, norm_c, norm_d)
        ffn[1].dve(dve, lambda a, d: None)
        final_dve(dve)

    ctx.close()


INPUTS = ["x_prompt", "x_sample", "cache_a_k", "cache_a_v", "state_ffn_conv", "ln_mix", "ln_ffn", "ln_final",
          "a_w_qkv", "a_rel_bias", "a_w_o", "b_w_in", "b_v_norm", "b_w_s", "b_bias_s", "b_w_out",
          "f_w_up", "f_conv_w", "f_conv_b", "f_w_down"]


def kernel(**inputs):
    import numpy as np
    import concourse.bacc as bacc
    from concourse.bass_utils import run_bass_kernel_spmd

    nc = bacc.Bacc("TRN2", target_bir_lowering=False, num_devices=1)
    arrays, args = {}, []
    for name in INPUTS:
        a = np.ascontiguousarray(inputs[name])
        arrays[f"in_{name}"] = a
        args.append(nc.dram_tensor(f"in_{name}", a.shape, mybir.dt.from_np(a.dtype), kind="ExternalInput").ap())
    (b, seq, d), (db, dec, _) = inputs["x_prompt"].shape, inputs["x_sample"].shape
    n_a, _, past, heads, hd = inputs["cache_a_k"].shape
    depth, ff2 = inputs["f_conv_b"].shape
    n_b = inputs["b_v_norm"].shape[0]
    keep = min(512, seq)
    shapes = [(b, seq, d), (db, dec, d), (n_a, b, keep, heads, hd), (n_a, b, keep, heads, hd),
              (n_a, db, dec, heads, hd), (n_a, db, dec, heads, hd), (n_b, db, dec, inputs["b_v_norm"].shape[1]),
              (depth, b, 2, ff2), (depth, db, 2, ff2)]
    for i, shape in enumerate(shapes):
        args.append(nc.dram_tensor(f"out_{i}", shape, F32, kind="ExternalOutput").ap())
    build(nc, *args)
    r = run_bass_kernel_spmd(nc, [arrays], core_ids=[0])
    return tuple(r.results[0][f"out_{i}"] for i in range(len(shapes)))
```

```python
from contextlib import ExitStack

import concourse.bass as bass
from concourse import mybir

F32 = mybir.dt.float32
F32R = mybir.dt.float32r
ALU = mybir.AluOpType
ACT = mybir.ActivationFunctionType
AX = mybir.AxisListType

P = 128
BANK = 512
EPS = 1e-6
NEG = -1e30


def build(nc, x_prompt, x_sample, cache_a_k, cache_a_v, state_ffn_conv, ln_mix, ln_ffn, ln_final,
          a_w_qkv, a_rel_bias, a_w_o, b_w_in, b_v_norm, b_w_s, b_bias_s, b_w_out,
          f_w_up, f_conv_w, f_conv_b, f_w_down,
          y_prompt, y_sample, new_k_prompt, new_v_prompt, new_k_sample, new_v_sample,
          new_gmlp_v, new_conv_prompt, new_conv_sample):
    SEQ, D = x_prompt.shape[1:]
    DEC = x_sample.shape[1]
    DEPTH = ln_mix.shape[0]
    HEADS, HD = cache_a_k.shape[3:]
    PAST = cache_a_k.shape[2]
    NREL = a_rel_bias.shape[2]
    MAXREL = NREL // 2
    KEEP = new_k_prompt.shape[2]
    GROUPS, MB = b_w_s.shape[1:3]
    FF = f_w_down.shape[1]

    KT = D // P
    GAP = 2
    TW = SEQ + GAP + DEC
    SMP = SEQ + GAP
    CH = [(0, 352), (352, 352), (704, TW - 704)]
    NCH = len(CH)
    NB = SEQ // P
    BLOCKS = [(P * b, P) for b in range(NB)] + [(SMP, DEC)]
    CK = 64
    BAND = 9 * CK
    VAR = 3 * CK
    REV = 2 * P + CK
    PAIRS = HEADS * HD // P
    FT = FF // P
    FIT = FT // 2
    CT = 2 * FT
    SCALE = HD ** -0.5
    QSCALE = 1.0 / SCALE
    assert HD == CK and FT % 2 == 0 and KEEP == 512 and PAST == 2 * P and MB == P

    ctx = ExitStack()

    def sem(name):
        return ctx.enter_context(nc.semaphore(name))

    def hold(name, shape, dt=F32):
        return ctx.enter_context(nc.sbuf_tensor(name, shape, dt))

    x = hold("x", [P, KT, TW])
    gx_hi = hold("gx_hi", [P, KT, TW], F32R)
    gx_lo = hold("gx_lo", [P, KT, TW], F32R)
    rstd = hold("rstd", [P, TW])
    ident = hold("ident", [P, P])
    ones = hold("ones", [P, P])
    gains = hold("gains", [P, 5 * KT])
    taps = [hold(f"taps{i}", [P, 6, CT]) for i in range(DEPTH)]
    raw0 = hold("raw0", [P, 2048])
    w_hi = [hold(f"w_hi{i}", [P, 1024], F32R) for i in range(2)]
    w_lo = [hold(f"w_lo{i}", [P, 1024], F32R) for i in range(2)]
    psum = ctx.enter_context(nc.psum_tensor("psum", [P, 8, BANK], F32))

    squares = hold("squares", [P, 2, 354])
    total = hold("total", [P, TW])
    rs_col = hold("rs_col", [P, NB + 1])

    def region(*allocs):
        with ExitStack() as local:
            return [local.enter_context(nc.sbuf_tensor(*a)) for a in allocs]

    xin, par_rows = region(("xin", [P, NB + 1, D], F32), ("par_rows", [P, 7, P], F32))
    (qd0, qd1, kT0, kT1, v0, v1, p_even, p_odd, pT, stage, o_hi, o_lo, bias, rel_tab, rel_rev, kc, vc,
     kcT, kout, neg_max, row_sum, row_inv) = region(
        ("qd0", [P, SEQ // CK + 1, P], F32), ("qd1", [P, SEQ // CK + 1, P], F32),
        ("kT0", [P, TW], F32), ("kT1", [P, TW], F32),
        ("v0", [P, NB + 1, P], F32), ("v1", [P, NB + 1, P], F32),
        ("p_even", [P, 5 * P], F32), ("p_odd", [P, 5 * P], F32), ("pT", [P, 2, 4 * P], F32),
        ("stage", [P, TW], F32), ("o_hi", [P, TW], F32R), ("o_lo", [P, TW], F32R),
        ("bias", [P, PAIRS, VAR], F32), ("rel_tab", [HEADS, NREL], F32), ("rel_rev", [HEADS, REV], F32),
        ("kc", [P, 2, P], F32), ("vc", [P, 2, P], F32), ("kcT", [P, PAST], F32), ("kout", [P, 5, P], F32),
        ("neg_max", [P, 2], F32), ("row_sum", [P, 2], F32), ("row_inv", [P, 2], F32))
    qd, kT, v_tok = [qd0, qd1], [kT0, kT1], [v0, v1]
    (raw1, w_hi2, w_hi3, w_lo2, w_lo3, a_gate, a_val, s_gate, h_hiA, h_hiB, h_loA, h_loB,
     conv_t, prod, cur, tails, tails_row) = region(
        ("raw1", [P, 2048], F32), ("w_hi2", [P, 1024], F32R), ("w_hi3", [P, 1024], F32R),
        ("w_lo2", [P, 1024], F32R), ("w_lo3", [P, 1024], F32R),
        ("a_gate", [P, TW + GAP], F32), ("a_val", [P, TW + GAP], F32), ("s_gate", [P, TW], F32),
        ("h_hiA", [P, TW], F32R), ("h_hiB", [P, TW], F32R), ("h_loA", [P, TW], F32R), ("h_loB", [P, TW], F32R),
        ("conv_t", [P, 2, 354], F32), ("prod", [P, 2, 354], F32), ("cur", [P, 6, 2, 2], F32),
        ("tails", [P, 4, CT], F32), ("tails_row", [P, 2, P], F32))
    a_buf, h_hi, h_lo = [a_gate, a_val], [h_hiA, h_hiB], [h_loA, h_loB]
    final_g, y2 = region(("final_g", [P, D], F32), ("y2", [P, D], F32))
    y_tile = [raw0[:, :D], raw0[:, D:], y2[:, :]]
    vT, vt0, vt1, wsT, bs, gain_v, gm_t, rc_v = region(
        ("vT", [P, KT, TW], F32), ("vt0", [P, KT, 2, P], F32), ("vt1", [P, KT, 2, P], F32),
        ("wsT", [P, GROUPS, P], F32), ("bs", [P, KT, P], F32), ("gain_v", [P, D], F32),
        ("gm_t", [P, 2, 354], F32), ("rc_v", [P, NB + 1], F32))
    v_pad = [vt0, vt1]
    f_hi, f_lo = w_hi + [w_hi2, w_hi3], w_lo + [w_lo2, w_lo3]
    bias_scratch = nc.dram_tensor("bias_scratch", [HEADS, CK, REV], F32, kind="Internal").ap()

    def at_least(engine, semaphore, value):
        if not isinstance(value, int) or value > 0:
            engine.wait_ge(semaphore, value)

    passed = sem("passed")

    def stand(engine):
        engine.sem_inc(passed, 1)

    def chunk(t, c):
        start, n = CH[c]
        return t[..., start:start + n]

    def product(pe, out, w, rhs, first, last):
        pe.matmul(out, w[0], rhs[0], start=first, stop=False)
        pe.matmul(out, w[0], rhs[1], start=False, stop=False)
        return pe.matmul(out, w[1], rhs[0], start=False, stop=last)

    def linear(pe, out, hi, lo, c, norm=None):
        for k in range(KT):
            if norm is not None:
                pe.wait_ge(Norm.lo, norm.tiles + KT * c + k + 1)
            cut = slice(k * P, (k + 1) * P)
            last = product(pe, out, (hi[:, cut], lo[:, cut]), (chunk(gx_hi[:, k, :], c), chunk(gx_lo[:, k, :], c)),
                           k == 0, k == KT - 1)
        return last

    def psum_pair(first_bank, n):
        if n <= BANK:
            return psum[:, first_bank, :n]
        return psum[:, first_bank:first_bank + 2, :n // 2]

    class Norm:

        def __init__(self, index, which, x_ready, split=True, bank=7):
            self.bank = bank
            self.which, self.x_ready, self.split = which, x_ready, split
            self.tiles, self.chunks, self.nth = KT * NCH * index, NCH * index, index - 1

        hi = sem("norm_hi")
        lo = sem("norm_lo")
        squared = sem("norm_squared")
        added = sem("norm_added")
        summed = sem("norm_summed")
        mean = sem("norm_mean")
        root = sem("norm_root")
        ready = sem("norm_rstd")
        c_sum = sem("norm_c_sum")
        c_mean = sem("norm_c_mean")
        c_root = sem("norm_c_root")
        c_inv = sem("norm_c_inv")
        c_diag = sem("norm_c_diag")
        c_spread = sem("norm_c_spread")
        c_ready = sem("norm_c_ready")

        def gain(self, d):
            return gains[:, self.which * KT + d:self.which * KT + d + 1]

        def act_tile(self, act, c, d):
            self.x_ready(act, c, d)
            if self.split:
                self.act_hi(act, c, d)
            k = KT * c + d
            at_least(act, self.added, self.tiles + k - 1)
            act.activation(squares[:, k % 2, :CH[c][1]], chunk(x[:, d, :], c), ACT.Square).then_inc(self.squared, 1)

        def act_hi(self, act, c, d):
            act.activation(chunk(gx_hi[:, d, :], c), chunk(x[:, d, :], c), ACT.Copy, scale=self.gain(d))\
                .then_inc(self.hi, 1)

        def dve_tile(self, dve, c, d):
            if self.split:
                dve.wait_ge(self.hi, self.tiles + KT * c + d + 1)
                dve.scalar_tensor_tensor(chunk(gx_lo[:, d, :], c), chunk(x[:, d, :], c), self.gain(d),
                                         chunk(gx_hi[:, d, :], c), ALU.mult, ALU.subtract).then_inc(self.lo, 1)

        def pool(self, pool, c):
            for d in range(KT):
                k = KT * c + d
                pool.wait_ge(self.squared, self.tiles + k + 1)
                sq = squares[:, k % 2, :CH[c][1]]
                if d == 0:
                    pool.tensor_copy(chunk(total, c), sq).then_inc(self.added, 1)
                else:
                    pool.wait_ge(self.added, self.tiles + k)
                    pool.tensor_tensor(chunk(total, c), chunk(total, c), sq, ALU.add).then_inc(self.added, 1)

        def pe_sum(self, pe, c):
            pe.wait_ge(self.added, self.tiles + KT * (c + 1))
            at_least(pe, self.mean, self.chunks + c)
            pe.matmul(psum[:, self.bank, :CH[c][1]], ones[:, :], chunk(total, c), start=True, stop=True)\
                .then_inc(self.summed, 1)

        def dve_mean(self, dve, c):
            dve.wait_ge(self.summed, self.chunks + c + 1)
            dve.tensor_scalar(chunk(rstd, c), psum[:, self.bank, :CH[c][1]], 1.0 / D, EPS, ALU.mult, ALU.add)\
                .then_inc(self.mean, 1)

        def act_root(self, act, c):
            act.wait_ge(self.mean, self.chunks + c + 1)
            act.activation(chunk(rstd, c), chunk(rstd, c), ACT.Sqrt).then_inc(self.root, 1)

        def dve_rstd(self, dve, c):
            dve.wait_ge(self.root, self.chunks + c + 1)
            dve.reciprocal(chunk(rstd, c), chunk(rstd, c)).then_inc(self.ready, 1)

        COLS = ((slice(0, P), slice(0, NB)), (slice(0, DEC), slice(NB, NB + 1)))
        SPREAD = ((0, SEQ // 2, P, 6), (SEQ // 2, SEQ, P, 7), (SMP, TW, DEC, 6))

        def pe_columns(self, pe):
            pe.wait_ge(self.added, self.tiles + KT * NCH)
            for b, (start, n) in enumerate(BLOCKS):
                mm = pe.matmul(psum[:n, 7, 2 * b:2 * b + 2], total[:, start:start + n], ones[:, 0:2],
                               start=True, stop=True)
            mm.then_inc(self.c_sum, 1)

        def dve_columns(self, dve):
            dve.wait_ge(self.c_sum, self.nth + 1)
            sums = psum[:, 7, :2 * (NB + 1)].rearrange("p (b i) -> p b i", i=2)
            for rows, cut in self.COLS:
                dve.tensor_scalar(rs_col[rows, cut], sums[rows, cut, 0], 1.0 / D, EPS, ALU.mult, ALU.add)\
                    .then_inc(self.c_mean, 1)
            for k, (rows, cut) in enumerate(self.COLS):
                dve.wait_ge(self.c_root, 2 * self.nth + k + 1)
                dve.reciprocal(rs_col[rows, cut], rs_col[rows, cut]).then_inc(self.c_inv, 1)
            dve.wait_ge(self.c_inv, 2 * self.nth + 2)
            for b, (start, n) in enumerate(BLOCKS):
                op = dve.tensor_scalar(total[:n, start:start + n], ident[:n, :n], rs_col[:n, b:b + 1], None, ALU.mult)
            op.then_inc(self.c_diag, 1)

        def act_roots(self, act):
            for k, (rows, cut) in enumerate(self.COLS):
                act.wait_ge(self.c_mean, 2 * self.nth + 2)
                act.activation(rs_col[rows, cut], rs_col[rows, cut], ACT.Sqrt).then_inc(self.c_root, 1)

        def pe_spread(self, pe, parts):
            for j in parts:
                a, b, n, bank = self.SPREAD[j]
                pe.wait_ge(self.c_diag, self.nth + 1)
                if j == 2:
                    pe.wait_ge(self.c_ready, 3 * self.nth + 1)
                pe.matmul(psum[:, bank, :b - a], ones[:n, :], total[:n, a:b], start=True, stop=True)\
                    .then_inc(self.c_spread, 1)

        def act_spread(self, act, parts):
            for j in parts:
                a, b, n, bank = self.SPREAD[j]
                act.wait_ge(self.c_spread, 3 * self.nth + j + 1)
                act.activation(rstd[:, a:b], psum[:, bank, :b - a], ACT.Copy).then_inc(self.c_ready, 1)

        def rstd_wait(self, engine, c):
            parts = max(j for j, (a, b, _, _) in enumerate(self.SPREAD) if a < CH[c][0] + CH[c][1])
            engine.wait_ge(self.c_ready, 3 * self.nth + parts + 1)

        def dve_row(self, dve, c):
            self.dve_mean(dve, c)
            self.dve_rstd(dve, c)
            dve.wait_ge(self.ready, self.chunks + c + 1)

    x_in = [sem(f"x_in{b}") for b in range(NB + 1)]
    gains_in = sem("gains_in")
    par_in = sem("par_in")
    consts = sem("consts")
    x_turned = sem("x_turned")
    x_act = sem("x_act")
    x_dve = sem("x_dve")
    par_turned = sem("par_turned")
    par_done = sem("par_done")
    LAST_BLOCK = [max(b for b in range(NB + 1) if BLOCKS[b][0] < CH[c][0] + CH[c][1]) for c in range(NCH)]
    FIRST = [(u, c) for c in range(NCH) for u in (0, 1)] + [(2, c) for c in range(NCH)]

    def x0_ready(engine, c, d):
        engine.wait_ge(x_act, LAST_BLOCK[c] + 1)
        engine.wait_ge(x_dve, LAST_BLOCK[c] + 1)
        if c == 0 and d == 0:
            engine.wait_ge(consts, 5)
            engine.wait_ge(par_done, 1)

    norm_a = Norm(0, 0, x0_ready, bank=4)

    def input_sp(sp):
        for b in range(0, NB, 2):
            sp.dma_start(xin[:, b, :], x_prompt[0, P * b:P * (b + 1), :]).then_inc(x_in[b], 16)
        sp.dma_start(xin[:DEC, NB, :], x_sample[0]).then_inc(x_in[NB], 16)

    def input_act_dma(act):
        act.dma_start(par_rows[:2 * KT, 0, :], ln_mix.rearrange("l (t p) -> (l t) p", p=P)).then_inc(gains_in, 16)
        act.dma_start(par_rows[2 * KT:4 * KT, 0, :], ln_ffn.rearrange("l (t p) -> (l t) p", p=P)).then_inc(gains_in, 16)
        act.dma_start(par_rows[4 * KT:5 * KT, 0, :], ln_final.rearrange("(t p) -> t p", p=P)).then_inc(gains_in, 16)
        for b in range(1, NB, 2):
            act.dma_start(xin[:, b, :], x_prompt[0, P * b:P * (b + 1), :]).then_inc(x_in[b], 16)
        for i in range(DEPTH):
            act.dma_start(par_rows[:2 * CT, 1 + 3 * i, :],
                          f_conv_w[i, 0:2].rearrange("j (t p) -> (j t) p", p=P)).then_inc(par_in, 16)
            act.dma_start(par_rows[:CT, 2 + 3 * i, :],
                          f_conv_w[i, 2].rearrange("(t p) -> t p", p=P)).then_inc(par_in, 16)
            act.dma_start(par_rows[CT:2 * CT, 2 + 3 * i, :],
                          f_conv_b[i].rearrange("(t p) -> t p", p=P)).then_inc(par_in, 16)
            act.dma_start(par_rows[:2 * CT, 3 + 3 * i, :],
                          state_ffn_conv[i, 0].rearrange("j (t p) -> (j t) p", p=P)).then_inc(par_in, 16)


    def input_pool(pool):
        pool.dma_start(rel_tab[:, :], a_rel_bias[0]).then_inc(rel_in, 16)
        pool.memset(rel_rev[:, 0:P], 0.0).then_inc(rel_done, 1)
        pool.memset(ident[:, :], 0.0).then_inc(consts, 1)
        pool.wait_ge(consts, 1)
        pool.affine_select(out=ident[:, :], in_=ident[:, :], compare_op=ALU.not_equal, fill=1.0, base=0,
                           pattern=[[-1, P]], channel_multiplier=1).then_inc(consts, 1)
        pool.memset(ones[:, :], 1.0).then_inc(consts, 1)
        pool.memset(rstd[:, SEQ:SMP], 0.0).then_inc(consts, 1)
        pool.memset(x[:, :, SEQ:SMP], 0.0).then_inc(consts, 1)
        pool.wait_ge(rel_done, 2)
        pool.dma_start(bias_scratch, rel_rev[:, None, :].to_broadcast([HEADS, CK, REV])).then_inc(rel_out, 16)
        pool.wait_ge(rel_out, 16)
        for h in range(2):
            src = bass.AP(bias_scratch.tensor, CK * REV * h + P - 1, [[REV - 1, CK], [2 * CK * REV, PAIRS], [1, VAR]])
            pool.dma_start(bias[CK * h:CK * (h + 1), :, :], src).then_inc(bias_in, 16)

    def turn_block(pe, b):
        n = BLOCKS[b][1]
        pe.wait_ge(x_in[b], 16)
        for half in range(2):
            at_least(pe, (x_act, x_dve)[half], b - 1)
            for j in range(4):
                d = 4 * half + j
                last = pe.transpose(psum[:, half + 2 * (b % 2), j * P:j * P + n],
                                    xin[:n, b, d * P:(d + 1) * P], ident[:n, :n])
            last.then_inc(x_turned, 1)

    def turned(b, half):
        start, n = BLOCKS[b]
        src = psum[:, half + 2 * (b % 2), :].rearrange("p (j n) -> p j n", j=4)[:, :, :n]
        return x[:, 4 * half:4 * half + 4, start:start + n], src

    def turn_params(pe, i):
        pe.wait_ge(consts, 2)
        if i == 0:
            pe.wait_ge(gains_in, 16 * 3)
            pe.transpose(psum[:, 5, :5 * KT], par_rows[:5 * KT, 0, :], ident[:5 * KT, :5 * KT]).then_inc(par_turned, 1)
            return
        pe.wait_ge(par_in, 16 * 4 * DEPTH)
        pe.wait_ge(par_done, i)
        n = 2 * CT
        for j in range(3):
            mm = pe.transpose(psum[:, 5, n * j:n * (j + 1)], par_rows[:n, 3 * (i - 1) + 1 + j, :], ident[:n, :n])
        mm.then_inc(par_turned, 1)

    def copy_params(act, i):
        act.wait_ge(par_turned, i + 1)
        if i == 0:
            dst, src = gains[:, :], psum[:, 5, :5 * KT]
        else:
            dst, src = taps[i - 1][:, :, :].rearrange("p j t -> p (j t)"), psum[:, 5, :6 * CT]
        act.activation(dst, src, ACT.Copy).then_inc(par_done, 1)

    def input_pe(pe):
        turn_params(pe, 0)
        for b in range(NB + 1):
            turn_block(pe, b)
            if b == LAST_BLOCK[1]:
                first_pe(pe, 0)
                norm_a.pe_sum(pe, 0)
                first_pe(pe, 1)

    def input_act(act):
        copy_params(act, 0)
        for b in range(NB + 1):
            act.wait_ge(x_turned, 2 * b + 1)
            act.activation(*turned(b, 0), ACT.Copy).then_inc(x_act, 1)
            if b in LAST_BLOCK:
                c = LAST_BLOCK.index(b)
                for d in range(KT):
                    norm_a.act_tile(act, c, d)
                    if (c, d) == (1, 3):
                        norm_a.act_root(act, 0)
                if c == 0:
                    split_act(act, 0)
                    split_act(act, 1)
        norm_a.act_root(act, 1)

    def input_dve(dve):
        dve.wait_ge(rel_in, 16)
        dve.tensor_scalar(rel_rev[:, P:], rel_tab[:, 2 * P - 1::-1][:, :REV - P], rel_tab[:, 2 * P:], None,
                          ALU.subtract).then_inc(rel_done, 1)
        for b in range(NB + 1):
            dve.wait_ge(x_turned, 2 * b + 2)
            dve.tensor_copy(*turned(b, 1)).then_inc(x_dve, 1)
            if b in LAST_BLOCK:
                c = LAST_BLOCK.index(b)
                for d in range(KT):
                    norm_a.dve_tile(dve, c, d)
                    if (c, d) == (1, 3):
                        norm_a.dve_mean(dve, 0)
                if c == 0:
                    split_dve(dve, 0)
                    split_dve(dve, 1)
                if c == 1:
                    norm_a.dve_rstd(dve, 0)
                    dve.wait_ge(Norm.ready, 1)
                    for o in range(2):
                        first_out(dve, o)

    QKV0 = 3
    at_raw = [sem(f"at_raw{i}") for i in range(2)]
    at_hi = sem("at_hi")
    at_lo = sem("at_lo")
    qkv_done = sem("qkv_done")
    oq_free = sem("oq_free")
    qk_done = sem("qk_done")
    biased = sem("biased")
    max_done = sem("max_done")
    exp_done = sem("exp_done")
    inv_done = sem("inv_done")
    p_done = sem("p_done")
    t_done = sem("t_done")
    t_free = sem("t_free")
    pv_done = sem("pv_done")
    o_hi_done = sem("o_hi_done")
    wo_done = sem("wo_done")
    at_added = sem("at_added")
    at_zero = sem("at_zero")
    p_zero = sem("p_zero")
    rel_in = sem("rel_in")
    rel_done = sem("rel_done")
    rel_out = sem("rel_out")
    bias_in = sem("bias_in")
    kc_in = sem("kc_in")
    vc_in = sem("vc_in")
    k_out = sem("k_out")
    v_out = sem("v_out")

    STEPS = NB + 1
    BURST = NCH * KT

    def key_blocks(s):
        return list(range(max(0, s - 4), s + 1)) if s < NB else list(range(3))

    def key_groups(s):
        blocks = key_blocks(s)
        return [blocks[i:i + 2] for i in range(0, len(blocks), 2)]

    PV_PAIR = sum(len(key_groups(s)) for s in range(STEPS))
    EXTRAS = {0: [("kc",)], 3: [("v", 0, 1, 2, 3)], 4: [("v", 4, 5, 6, 7)], 5: [("v", 8)],
              6: [("k", 4, 5, 6, 7)], 7: [("k", 8)]}
    T_FIRST = sum(len(e) for e in EXTRAS.values()) - 1
    V_FIRST = sum(len(EXTRAS[s]) for s in (3, 4, 5))
    T_PAIR = PV_PAIR + T_FIRST + 1
    assert T_PAIR % 2 == 0

    def extras(s, cached, following):
        return [e for e in EXTRAS.get(s, []) if (cached if e[0] == "kc" else following)]

    class Plan:

        def __init__(self, following):
            self.oq, self.o, self.q, n = [], {}, {}, 0
            for s in range(STEPS + 1):
                if s:
                    self.o[s - 1] = n
                    n += 1
                if s < STEPS and following:
                    self.q[s] = n
                    n += 1
            self.n_oq = n
            self.t, self.extra, self.pv, n, m, users = {}, {}, {}, 0, 0, {}
            for s in range(STEPS + 1):
                if s:
                    for g in range(len(key_groups(s - 1))):
                        slot = (T_FIRST + n) % 2
                        self.t[s - 1, g] = (n, m, users.get(slot, 0))
                        users[slot] = m + 1
                        n, m = n + 1, m + 1
                if s < STEPS:
                    for e in extras(s, True, following):
                        self.extra[s, e] = n
                        n += 1

    PLAN = {f: Plan(f) for f in (False, True)}
    OQ_FIRST, OQ_PAIR = STEPS, PLAN[True].n_oq
    assert OQ_PAIR % 2 == 0

    def chunk_scores(s, odd):
        if s == NB:
            return 0, PAST + DEC
        c = 2 * s + odd
        return CK * max(0, c - 8), CK * (min(c, 8) + 1)

    def scores_of(s, odd):
        return psum_pair(2 * odd, chunk_scores(s, odd)[1])

    def chunks_of(s):
        return [0, 1] if s < NB else [0]

    def split_act(act, n):
        act.wait_ge(at_raw[n % 2], 16 * (n // 2 + 1))
        act.activation(w_hi[n % 2][:, :], raw0[:, 1024 * (n % 2):1024 * (n % 2) + 1024], ACT.Copy).then_inc(at_hi, 1)

    def split_dve(dve, n):
        dve.wait_ge(at_hi, n + 1)
        dve.tensor_tensor(w_lo[n % 2][:, :], raw0[:, 1024 * (n % 2):1024 * (n % 2) + 1024], w_hi[n % 2][:, :],
                          ALU.subtract).then_inc(at_lo, 1)

    class Unit:

        def __init__(self, t, par, k):
            self.slot = (QKV0 + 4 * par + k) % 2
            self.count = QKV0 + 4 * t + k + 1
            self.loads = 2 * t + (QKV0 + k) // 2 + 1

        def act(self, act):
            act.wait_ge(at_raw[self.slot], 16 * self.loads)
            act.activation(w_hi[self.slot][:, :], raw0[:, 1024 * self.slot:1024 * self.slot + 1024], ACT.Copy)\
                .then_inc(at_hi, 1)

        def dve(self, dve):
            dve.wait_ge(at_hi, self.count)
            dve.tensor_tensor(w_lo[self.slot][:, :], raw0[:, 1024 * self.slot:1024 * self.slot + 1024],
                              w_hi[self.slot][:, :], ALU.subtract).then_inc(at_lo, 1)

    def load_unit(sp, n_mod, count, src):
        at_least(sp, at_lo, count - 2)
        if not isinstance(count, int):
            stand(sp)
        raw = raw0[:, 1024 * n_mod:1024 * n_mod + 1024]
        if src.shape[0] != P:
            src = src.rearrange("(k p) n -> p k n", p=P)
            raw = raw.rearrange("p (k n) -> p k n", k=KT)
        sp.dma_start(raw, src).then_inc(at_raw[n_mod], 16)

    def qkv_unit(which, t):
        return a_w_qkv[0, :, bass.ds(D * which + P * t, P)]

    def attention_sp(sp):
        def pair(t, par, units):
            for k in units:
                src = {0: lambda: qkv_unit(2, t + 1), 1: lambda: qkv_unit(1, t + 1), 2: lambda: qkv_unit(0, t + 1),
                       3: lambda: a_w_o[0, bass.ds(P * t, P), :], 4: lambda: qkv_unit(2, t + 2)}[k]()
                load_unit(sp, (QKV0 + k) % 2, QKV0 + 4 * t + k + 1, src)

        load_unit(sp, QKV0 % 2, QKV0 + 1, qkv_unit(2, 1))
        with sp.Fori(0, PAIRS // 2 - 1) as j:
            pair(2 * j, 0, [1, 2, 3, 4])
            pair(2 * j + 1, 1, [1, 2, 3, 4])
        pair(PAIRS - 2, 0, [1, 2, 3])
        load_unit(sp, (QKV0 + 4) % 2, QKV0 + 4 * (PAIRS - 2) + 5, a_w_o[0, P * (PAIRS - 1):, :])

    def attention_first_sp(sp):
        for n, which in enumerate([2, 1]):
            load_unit(sp, n, n + 1, qkv_unit(which, 0))

    def attention_second_sp(sp):
        load_unit(sp, 0, 3, qkv_unit(0, 0))

    def attention_pool(pool):
        pool.wait_ge(x_act, NB + 1)
        pool.wait_ge(x_dve, NB + 1)
        for t in (qd0, qd1):
            pool.memset(t[:, :, :], 0.0).then_inc(at_zero, 1)
        pool.wait_ge(par_done, 1 + DEPTH)
        pool.memset(p_even[:, BAND:], 0.0).then_inc(at_zero, 1)
        pool.memset(p_odd[:, :CK], 0.0).then_inc(at_zero, 1)
        for t in (o_hi, o_lo):
            pool.memset(t[:, SEQ:SMP].bitcast(F32), 0.0).then_inc(at_zero, 1)

        def load_cache(t):
            for src, dst, done in ((cache_a_k, kc, kc_in), (cache_a_v, vc, vc_in)):
                flat = src[0, 0].rearrange("(b p) h e -> p b (h e)", p=P)
                pool.dma_start(dst[:, :, :], flat[:, :, bass.ds(P * t, P)]).then_inc(done, 16)

        def store(t, par, t_count, v_count):
            if v_count is not None:
                pool.wait_ge(t_free, v_count)
                stand(pool)
                pool.dma_start(new_v_prompt[0, 0].rearrange("(b p) h e -> p b (h e)", p=P)[:, :, bass.ds(P * t, P)],
                               v_tok[par][:, NB - 4:NB, :]).then_inc(v_out, 16)
                pool.dma_start(new_v_sample[0, 0].rearrange("p h e -> p (h e)")[:, bass.ds(P * t, P)],
                               v_tok[par][:DEC, NB, :]).then_inc(v_out, 16)
            pool.wait_ge(t_free, t_count)
            stand(pool)
            pool.dma_start(new_k_prompt[0, 0].rearrange("(b p) h e -> p b (h e)", p=P)[:, :, bass.ds(P * t, P)],
                           kout[:, :4, :]).then_inc(k_out, 16)
            pool.dma_start(new_k_sample[0, 0].rearrange("p h e -> p (h e)")[:, bass.ds(P * t, P)],
                           kout[:DEC, 4, :]).then_inc(k_out, 16)

        load_cache(0)
        store(0, 0, 2 + T_FIRST, 2 + V_FIRST)

        def pair(t, par, following):
            plan = PLAN[following]
            base = T_FIRST + T_PAIR * t
            for s in range(4):
                pool.wait_ge(qk_done, (2 * NB + 1) * t + 2 * s + 1)
                stand(pool)
                pool.memset(p_even[:, P * s + CK:P * (s + 1)], 0.0).then_inc(p_zero, 1)
            if following:
                store(t + 1, 1 - par, 2 + base + plan.extra[7, ("k", 8)] + 1, 2 + base + plan.extra[5, ("v", 8)] + 1)
                pool.wait_ge(pv_done, 1 + PV_PAIR * (t + 1))
                stand(pool)
                load_cache(t + 1)

        with pool.Fori(0, PAIRS // 2 - 1) as j:
            pair(2 * j, 0, True)
            pair(2 * j + 1, 1, True)
        pair(PAIRS - 2, 0, True)
        pair(PAIRS - 1, 1, False)

    def extra_pe(pe, e, par_next, slot):
        out = psum[:, 4 + slot, :]
        for j, b in enumerate(e[1:] if e[0] != "kc" else (0, 1)):
            if e[0] == "kc":
                last = pe.transpose(out[:, P * j:P * (j + 1)], kc[:, b, :], ident[:, :])
            else:
                start, n = BLOCKS[b]
                src = stage if e[0] == "v" else kT[par_next]
                last = pe.transpose(out[:n, P * j:P * (j + 1)], src[:, start:start + n], ident[:, :])
        last.then_inc(t_done, 1)

    def extra_act(act, e, par_next, slot):
        out = psum[:, 4 + slot, :]
        if e[0] == "kc":
            dst, src = kcT[:, :], out[:, :PAST]
        else:
            first, n, m = e[1], BLOCKS[e[1]][1], len(e) - 1
            src = out[:n, :P * m].rearrange("p (b n) -> p b n", n=P)
            dst = v_tok[par_next][:n, first:first + m, :] if e[0] == "v" else kout[:n, first - 4:first - 4 + m, :]
        act.activation(dst, src, ACT.Copy).then_inc(t_free, 1)

    def qkv_pe(pe, u, c, bank, unit_count, slot, norm=None):
        pe.wait_ge(at_lo, unit_count)
        linear(pe, psum[:, bank, :CH[c][1]], w_hi[slot], w_lo[slot], c, norm).then_inc(qkv_done, 1)

    def first_pe(pe, o):
        u, c = FIRST[o]
        pe.wait_ge(oq_free, o + 1)
        qkv_pe(pe, u, c, 6 + o % 2, u + 1, u % 2, norm_a if u == 0 else None)

    def attention_pe(pe):
        for o in range(2, STEPS):
            first_pe(pe, o)
            if o in (3, 4):
                norm_a.pe_sum(pe, o - 2)
            if o in (4, 5):
                turn_params(pe, o - 3)
            if o == 5:
                pe.wait_ge(par_done, 1 + DEPTH)
                pe.wait_ge(oq_free, 2 + 5)
                for n, e in enumerate([e for s in (3, 4, 5) for e in EXTRAS[s]]):
                    pe.wait_ge(t_free, n + 1)
                    extra_pe(pe, e, 0, n % 2)
        pe.wait_ge(oq_free, 2 + 6)
        for n, e in enumerate([e for s in (6, 7) for e in EXTRAS[s]]):
            pe.wait_ge(t_free, V_FIRST + n + 1)
            extra_pe(pe, e, 0, (V_FIRST + n) % 2)

        def values(t, par, s, plan, part):
            bank = 6 + (OQ_FIRST + plan.o[s]) % 2
            blocks = key_blocks(s)
            if part == 0:
                pe.wait_ge(p_done, (2 * NB + 1) * t + 2 * s + len(chunks_of(s)))
                if s < 4:
                    pe.wait_ge(p_zero, 4 * t + s + 1)

            def turn(g, group):
                n, m, _ = plan.t[s, g]
                slot = (T_FIRST + n) % 2
                pe.wait_ge(t_free, T_FIRST + T_PAIR * t + n + 1)
                for i, kb in enumerate(group):
                    rows = P if s < NB or kb < 2 else DEC
                    for odd in chunks_of(s):
                        at = P * (kb - blocks[0]) + (CK if odd and s < 4 else 0)
                        src = (p_even, p_odd)[odd][:, at:at + rows]
                        last = pe.transpose(psum[:rows, 4 + slot, P * (2 * i + odd):P * (2 * i + odd + 1)],
                                            src, ident[:, :])
                last.then_inc(t_done, 1)

            def weigh(g, group):
                n, m, _ = plan.t[s, g]
                slot = (T_FIRST + n) % 2
                width = 2 * P if s < NB else P
                pe.wait_ge(t_free, 2 + T_FIRST + T_PAIR * t + n + 1)
                if g == 0:
                    pe.wait_ge(oq_free, OQ_FIRST + OQ_PAIR * t + plan.o[s] + 1)
                    if s == NB:
                        pe.wait_ge(vc_in, 16 * (t + 1))
                for i, kb in enumerate(group):
                    rows = P if s < NB or kb < 2 else DEC
                    v = v_tok[par][:rows, kb if s < NB else NB, :] if s < NB or kb == 2 else vc[:, kb, :]
                    mm = pe.matmul(psum[:, bank, :width], v, pT[:rows, slot, 2 * P * i:2 * P * i + width],
                                   start=(kb == blocks[0]), stop=(kb == blocks[-1]))
                mm.then_inc(pv_done, 1)

            groups = key_groups(s)
            if part == 0:
                for g in range(min(2, len(groups))):
                    turn(g, groups[g])
                return
            for g in range(len(groups)):
                weigh(g, groups[g])
                if g + 2 < len(groups):
                    turn(g + 2, groups[g + 2])

        def pair(t, par, following):
            plan = PLAN[following]
            base = T_FIRST + T_PAIR * t
            pe.wait_ge(oq_free, 2 + OQ_PAIR * t + OQ_FIRST)
            pe.wait_ge(at_added, BURST * t + 1)
            for s in range(STEPS + 1):
                if s:
                    values(t, par, s - 1, plan, 0)
                for odd in chunks_of(s) if s < STEPS else []:
                    q = (2 * NB + 1) * t + 2 * s + odd
                    if s:
                        pe.wait_ge(exp_done, (2 * NB + 1) * t + 2 * (s - 1) + odd + 1)
                    first, n = chunk_scores(s, odd)
                    stat = qd[par][:, 2 * s + odd, :]
                    if s == NB:
                        pe.wait_ge(t_free, 2 + base + plan.extra[0, ("kc",)] + 1)
                        pe.matmul(psum[:, 0, :PAST], stat, kcT[:, :], start=True, stop=True)
                        last = pe.matmul(psum[:, 0, PAST:n], stat, kT[par][:, SMP:], start=True, stop=True)
                    elif n <= BANK:
                        last = pe.matmul(psum[:, 2 * odd, :n], stat, kT[par][:, first:first + n], start=True, stop=True)
                    else:
                        for i in range(2):
                            last = pe.matmul(psum[:, 2 * odd + i, :n // 2], stat,
                                             kT[par][:, first + i * n // 2:first + (i + 1) * n // 2],
                                             start=True, stop=True)
                    last.then_inc(qk_done, 1)
                if s:
                    values(t, par, s - 1, plan, 1)
                if s == STEPS:
                    break
                if following:
                    u, c = divmod(s, NCH)
                    k = OQ_FIRST + plan.q[s]
                    pe.wait_ge(oq_free, OQ_PAIR * t + k + 1)
                    qkv_pe(pe, u, c, 6 + k % 2, QKV0 + 4 * t + u + 1, (QKV0 + u) % 2)
                for e in extras(s, True, following):
                    n = plan.extra[s, e]
                    pe.wait_ge(t_free, base + n + 1)
                    if e[0] == "kc":
                        pe.wait_ge(kc_in, 16 * (t + 1))
                    elif e[0] == "v" and s == 3:
                        pe.wait_ge(oq_free, 2 + OQ_FIRST + OQ_PAIR * t + plan.q[2] + 1)
                    elif s == 6:
                        pe.wait_ge(oq_free, 2 + OQ_FIRST + OQ_PAIR * t + plan.q[5] + 1)
                    extra_pe(pe, e, 1 - par, (T_FIRST + n) % 2)
            k = 3 if following else 0
            slot = (QKV0 + k) % 2
            pe.wait_ge(at_lo, QKV0 + 4 * t + k + 1)
            for n in range(BURST):
                c, d = divmod(n, KT)
                if d == 0:
                    pe.wait_ge(oq_free, 2 + OQ_FIRST + OQ_PAIR * t + plan.o[LAST_BLOCK[c]] + 1)
                if n >= 4:
                    pe.wait_ge(at_added, BURST * t + n - 3 + 1)
                cut = slice(P * d, P * (d + 1))
                product(pe, psum[:, n % 4, :CH[c][1]], (w_hi[slot][:, cut], w_lo[slot][:, cut]),
                        (chunk(o_hi[:, :], c), chunk(o_lo[:, :], c)), True, True).then_inc(wo_done, 1)

        with pe.Fori(0, PAIRS // 2 - 1) as j:
            pair(2 * j, 0, True)
            pair(2 * j + 1, 1, True)
        pair(PAIRS - 2, 0, True)
        pair(PAIRS - 1, 1, False)

    def o_halves(s, tensor, par_bank):
        start, n = BLOCKS[s]
        for h in range(2):
            rows = slice(CK * h, CK * (h + 1))
            if s < NB:
                dst = tensor[rows, start:start + n].rearrange("p (c q) -> p c q", q=CK)
                src = psum[rows, par_bank, :2 * P].rearrange("p (c h q) -> p c h q", h=2, q=CK)[:, :, h, :]
            else:
                dst = tensor[rows, start:start + n]
                src = psum[rows, par_bank, CK * h:CK * h + DEC]
            yield dst, src

    def attention_act(act, norm):
        norm_a.act_root(act, 2)
        act.wait_ge(qkv_done, 5)
        split_act(act, 2)
        for i in range(1, 1 + DEPTH):
            copy_params(act, i)
        act.wait_ge(qkv_done, 6)
        split_act(act, 3)
        firsts = [e for s in (3, 4, 5, 6, 7) for e in EXTRAS[s]]
        for n, e in enumerate(firsts):
            act.wait_ge(t_done, n + 1)
            extra_act(act, e, 0, n % 2)

        def pair(half, par, following, again):
            t = 2 * half + par
            plan = PLAN[following]
            base = T_FIRST + T_PAIR * t
            tiles = (2 * NB + 1) * t
            for s in range(STEPS + 1):
                if s:
                    groups = key_groups(s - 1)
                    for g, group in enumerate(groups):
                        n, m, before = plan.t[s - 1, g]
                        slot = (T_FIRST + n) % 2
                        rows = P if s - 1 < NB or group[0] < 2 else DEC
                        width = 2 * P if s - 1 < NB else P
                        act.wait_ge(t_done, base + n + 1)
                        act.wait_ge(pv_done, 1 + PV_PAIR * t + before)
                        dst, src = (v[:rows].rearrange("p (i n) -> p i n", i=2)[:, :len(group), :width]
                                    for v in (pT[:, slot, :], psum[:, 4 + slot, :]))
                        act.activation(dst, src, ACT.Copy).then_inc(t_free, 1)
                    bank = 6 + (OQ_FIRST + plan.o[s - 1]) % 2
                    act.wait_ge(pv_done, 1 + PV_PAIR * t + plan.t[s - 1, len(groups) - 1][1] + 1)
                    for dst, src in o_halves(s - 1, o_hi, bank):
                        act.activation(dst, src, ACT.Copy).then_inc(o_hi_done, 1)
                if s == STEPS:
                    break
                if s == 0:
                    act.wait_ge(wo_done, BURST * t + 1)
                    act.wait_ge(qkv_done, STEPS * (t + 1))
                    Unit(t, par, 1 if following else 0).act(act)
                elif following and s == 3:
                    act.wait_ge(qkv_done, STEPS * (t + 1) + 3)
                    Unit(t, par, 2).act(act)
                elif following and s == 6:
                    act.wait_ge(qkv_done, STEPS * (t + 1) + 6)
                    Unit(t, par, 3).act(act)
                for odd in chunks_of(s):
                    q = 2 * s + odd
                    first, n = chunk_scores(s, odd)
                    act.wait_ge(max_done, tiles + q + 1)
                    dst = p_even[:, :n] if not odd else p_odd[:, CK:CK + n]
                    if n > BANK:
                        dst = dst.rearrange("p (i n) -> p i n", i=2)
                    act.activation(dst, scores_of(s, odd), ACT.Exp, bias=neg_max[:, odd:odd + 1],
                                   accum_out=row_sum[:, odd:odd + 1]).then_inc(exp_done, 1)
                for e in extras(s, True, following):
                    n = plan.extra[s, e]
                    act.wait_ge(t_done, base + n + 1)
                    if e == ("v", 0, 1, 2, 3):
                        act.wait_ge(v_out, 32 * (t + 1))
                    elif e == ("k", 4, 5, 6, 7):
                        act.wait_ge(k_out, 32 * (t + 1))
                    extra_act(act, e, 1 - par, (T_FIRST + n) % 2)
            if again:
                act.wait_ge(qkv_done, STEPS * (t + 1) + 9)
                Unit(t, par, 4).act(act)

        with act.Fori(0, PAIRS // 2 - 1) as j:
            pair(j, 0, True, True)
            pair(j, 1, True, True)
        pair(PAIRS // 2 - 1, 0, True, False)
        pair(PAIRS // 2 - 1, 1, False, False)
        ffn[0].split(act, None, 0, 0)
        for c in range(NCH):
            for d in range(KT):
                norm.act_tile(act, c, d)
        act.wait_ge(wo_done, 1 + BURST * PAIRS)

    def first_out(dve, o):
        dve.wait_ge(qkv_done, o + 1)
        qkv_out(dve, *FIRST[o], 6 + o % 2, 0)

    def qkv_out(dve, u, c, bank, par):
        start, n = CH[c]
        src, r = psum[:, bank, :n], rstd[:, start:start + n]
        if u < 2:
            dst = chunk((stage, kT[par])[u], c)
            dve.tensor_tensor(dst, src, r, ALU.mult).then_inc(oq_free, 1)
            return
        cuts, at = [], start
        while at < start + n:
            if at == SEQ:
                at = SMP
            end = start + n if at >= SMP else min(start + n, SEQ, (at // CK + 1) * CK)
            if at < SMP and at % CK == 0:
                end = max(end, min(start + n, SEQ) // CK * CK)
            cuts.append((at, end))
            at = end
        for at, end in cuts:
            i, j = (SEQ // CK, 0) if at >= SMP else divmod(at, CK)
            m = end - at
            for h in range(2):
                rows = slice(CK * h, CK * (h + 1))
                a, b = src[rows, at - start:end - start], r[rows, at - start:end - start]
                if m > CK:
                    dst = qd[par][rows, i:i + m // CK, CK * h:CK * (h + 1)]
                    a, b = (v.rearrange("p (c q) -> p c q", q=CK) for v in (a, b))
                else:
                    dst = qd[par][rows, i, CK * h + j:CK * h + j + m]
                last = dve.scalar_tensor_tensor(dst, a, SCALE, b, ALU.mult, ALU.mult)
        last.then_inc(oq_free, 1)

    def attention_dve(dve, norm):
        norm_a.dve_row(dve, 1)
        for o in range(2, STEPS):
            if o == 4:
                norm_a.dve_row(dve, 2)
            if o == 6:
                dve.wait_ge(at_zero, 2)
                split_dve(dve, 3)
            first_out(dve, o)
            if o == 4:
                split_dve(dve, 2)
        dve.wait_ge(bias_in, 32)
        dve.wait_ge(at_zero, 6)

        def pair(half, par, following, again):
            t = 2 * half + par
            plan = PLAN[following]
            tiles = (2 * NB + 1) * t
            for s in range(STEPS + 1):
                for odd in chunks_of(s) if s < STEPS else []:
                    q = tiles + 2 * s + odd
                    first, n = chunk_scores(s, odd)
                    dve.wait_ge(qk_done, q + 1)
                    if s == NB:
                        part, b = psum[:, 0, PAST - P:n], bias[:, t, 0:P + DEC]
                    elif n > BANK:
                        part, b = psum[:, 2 * odd + 1, n // 2 - VAR:n // 2], bias[:, t, :]
                    else:
                        m = min(n, VAR)
                        part, b = psum[:, 2 * odd, n - m:n], bias[:, t, VAR - m:]
                    dve.tensor_tensor(part, part, b, ALU.add).then_inc(biased, 1)
                    dve.wait_ge(biased, q + 1)
                    dve.tensor_reduce(neg_max[:, odd:odd + 1], scores_of(s, odd), AX.XY if n > BANK else AX.X,
                                      ALU.max, negate=True).then_inc(max_done, 1)
                if s:
                    bank = 6 + (OQ_FIRST + plan.o[s - 1]) % 2
                    dve.wait_ge(o_hi_done, 2 * STEPS * t + 2 * s)
                    for (dst, src), (hi, _) in zip(o_halves(s - 1, o_lo, bank), o_halves(s - 1, o_hi, bank)):
                        last = dve.tensor_tensor(dst, src, hi, ALU.subtract)
                    last.then_inc(oq_free, 1)
                if s == STEPS:
                    break
                if s == 0:
                    Unit(t, par, 1 if following else 0).dve(dve)
                elif following and s in (3, 6):
                    Unit(t, par, s // 3 + 1).dve(dve)
                for odd in chunks_of(s):
                    q = tiles + 2 * s + odd
                    n = chunk_scores(s, odd)[1]
                    dve.wait_ge(exp_done, q + 1)
                    dve.reciprocal(row_inv[:, odd:odd + 1], row_sum[:, odd:odd + 1]).then_inc(inv_done, 1)
                    dve.wait_ge(inv_done, q + 1)
                    p = p_even[:, :n] if not odd else p_odd[:, CK:CK + n]
                    dve.tensor_scalar(p, p, row_inv[:, odd:odd + 1], None, ALU.mult).then_inc(p_done, 1)
                if following:
                    u, c = divmod(s, NCH)
                    dve.wait_ge(qkv_done, STEPS * (t + 1) + s + 1)
                    qkv_out(dve, u, c, 6 + (OQ_FIRST + plan.q[s]) % 2, 1 - par)
            if again:
                Unit(t, par, 4).dve(dve)
            elif not following:
                ffn[0].split(None, dve, 0, 0)
            dve.wait_ge(at_added, BURST * t + 1)
            for n in range(BURST):
                c, d = divmod(n, KT)
                dve.wait_ge(wo_done, 1 + BURST * t + n + 1)
                dve.tensor_tensor(chunk(x[:, d, :], c), chunk(x[:, d, :], c), psum[:, n % 4, :CH[c][1]], ALU.add)\
                    .then_inc(at_added, 1)
                if not following and c:
                    norm.dve_tile(dve, c - 1, d)

        with dve.Fori(0, PAIRS // 2 - 1) as j:
            pair(j, 0, True, True)
            pair(j, 1, True, True)
        pair(PAIRS // 2 - 1, 0, True, False)
        pair(PAIRS // 2 - 1, 1, False, False)
        for d in range(KT):
            norm.dve_tile(dve, NCH - 1, d)

    DOWN = NCH * KT
    UP = 4 * NCH
    RING = 6
    WEIGHTS = 6

    class Ffn:

        gate_in = sem("ffn_gate_in")
        value_in = sem("ffn_value_in")
        down_in = sem("ffn_down_in")
        w_hi = sem("ffn_w_hi")
        w_lo = sem("ffn_w_lo")
        up = sem("ffn_up")
        down = sem("ffn_down")
        free = sem("ffn_free")
        added = sem("ffn_added")
        affine = sem("ffn_affine")
        conv1 = sem("ffn_conv1")
        conv = sem("ffn_conv")
        silu = sem("ffn_silu")
        prod = sem("ffn_prod")
        h_hi = sem("ffn_h_hi")
        h_lo = sem("ffn_h_lo")
        edge = sem("ffn_edge")
        cur = sem("ffn_cur")
        hist = sem("ffn_hist")
        tail = sem("ffn_tail")
        tails_turned = sem("ffn_tails_turned")
        tails_row = sem("ffn_tails_row")
        tails_out = sem("ffn_tails_out")

        def __init__(self, layer, norm_in, norm_out):
            self.layer, self.norm_in, self.norm_out = layer, norm_in, norm_out
            self.norm_at = ((3, 4, 5), (2, 3, 4))[layer]
            self.done = FIT * layer

        def up_src(self, value, it):
            return f_w_up[self.layer, :, bass.ds(FF * value + 2 * P * it, 2 * P)].rearrange("(k p) n -> p k n", p=P)

        def down_src(self, it):
            return f_w_down[self.layer, bass.ds(2 * P * it, 2 * P), :].rearrange("(i p) n -> p i n", p=P)

        def sp_first(self, sp):
            sp.dma_start(raw0[:, :].rearrange("p (k n) -> p k n", k=KT), self.up_src(0, 0)).then_inc(self.gate_in, 16)

        def sp(self, sp, region_free, next_load):
            region_free(sp)
            sp.dma_start(raw1[:, :].rearrange("p (k n) -> p k n", k=KT), self.up_src(1, 0)).then_inc(self.value_in, 16)

            def iteration(it, last):
                done = self.done + it
                sp.wait_ge(self.w_lo, WEIGHTS * done + 3)
                stand(sp)
                sp.dma_start(raw0[:, :].rearrange("p (i n) -> p i n", i=2), self.down_src(it)).then_inc(self.down_in, 16)
                if not last:
                    sp.wait_ge(self.w_lo, WEIGHTS * done + 4)
                    stand(sp)
                    sp.dma_start(raw1[:, :].rearrange("p (k n) -> p k n", k=KT), self.up_src(1, it + 1))\
                        .then_inc(self.value_in, 16)
                    sp.wait_ge(self.w_lo, WEIGHTS * done + 6)
                    stand(sp)
                    sp.dma_start(raw0[:, :].rearrange("p (k n) -> p k n", k=KT), self.up_src(0, it + 1))\
                        .then_inc(self.gate_in, 16)

            iteration(0, False)
            with sp.Fori(1, FIT - 1) as it:
                iteration(it, False)
            iteration(FIT - 1, True)
            next_load(sp)
            sp.wait_ge(self.tails_row, 2 * self.layer + 2)
            for i, dst in enumerate((new_conv_prompt, new_conv_sample)):
                sp.dma_start(dst[self.layer, 0].rearrange("j (t p) -> (j t) p", p=P), tails_row[:2 * CT, i, :])\
                    .then_inc(self.tails_out, 16)

        def raw_of(self, u):
            if u >= 4:
                return raw0[:, 1024 * (u - 4):1024 * (u - 3)]
            both = (raw0, raw1)[u % 2][:, :].rearrange("p (k i n) -> p k i n", k=KT, i=2)
            return both[:, :, u // 2, :]

        def slot_of(self, u):
            return u % 2 if u < 4 else u - 2

        def split(self, act, dve, it, u):
            slot, done = self.slot_of(u), self.done + it
            count = WEIGHTS * done + u + 1
            shape = (lambda w: w[:, :]) if u >= 4 else (lambda w: w[:, :].rearrange("p (k n) -> p k n", k=KT))
            if act is not None:
                act.wait_ge((self.gate_in, self.value_in, self.gate_in, self.value_in, self.down_in, self.down_in)[u],
                            16 * (done + 1))
                if u >= 4:
                    pass
                elif u >= 2:
                    act.wait_ge(self.up, UP * done + NCH * (u - 1))
                else:
                    at_least(act, self.up, UP * done - UP + NCH * (u + 3))
                act.activation(shape(f_hi[slot]), self.raw_of(u), ACT.Copy).then_inc(self.w_hi, 1)
            else:
                dve.wait_ge(self.w_hi, count)
                dve.tensor_tensor(shape(f_lo[slot]), self.raw_of(u), shape(f_hi[slot]), ALU.subtract)\
                    .then_inc(self.w_lo, 1)

        SPLITS = {3: 2, 6: 3, 7: 4, 8: 5}
        NEXT_SPLITS = {2: 0, 7: 1}

        def pe(self, pe, banks_free, beside=lambda e, n: None):
            ring = RING

            def iteration(it, first, last):
                done = self.done + it
                for o in range(UP):
                    u, c = divmod(o, NCH)
                    if first and o in self.norm_at:
                        stage = self.norm_at.index(o)
                        if stage == 0:
                            self.norm_in.pe_columns(pe)
                        else:
                            self.norm_in.pe_spread(pe, ((0, 1), (2,))[stage - 1])
                    if c == 0:
                        pe.wait_ge(self.w_lo, WEIGHTS * done + u + 1)
                    if o >= RING:
                        pe.wait_ge(self.free, RING + UP * done + o - RING + 1)
                    elif first:
                        banks_free(pe, o)
                    else:
                        pe.wait_ge(self.added, DOWN * done - RING + o + 1)
                    linear(pe, psum[:, o % ring, :CH[c][1]], f_hi[u % 2], f_lo[u % 2], c,
                           self.norm_in if first and u == 0 else None).then_inc(self.up, 1)
                for n in range(DOWN):
                    c, d = divmod(n, KT)
                    if last:
                        beside(pe, n)
                    if n == 0:
                        pe.wait_ge(self.w_lo, WEIGHTS * done + 6)
                    if d == 0:
                        pe.wait_ge(self.h_lo, 2 * NCH * done + NCH + c + 1)
                    if n >= RING:
                        pe.wait_ge(self.added, DOWN * done + n - RING + 1)
                    else:
                        pe.wait_ge(self.free, RING + UP * (done + 1) - RING + n + 1)
                    cut = slice(P * d, P * (d + 1))
                    for i in range(2):
                        mm = product(pe, psum[:, n % ring, :CH[c][1]], (f_hi[2 + i][:, cut], f_lo[2 + i][:, cut]),
                                     (chunk(h_hi[i][:, :], c), chunk(h_lo[i][:, :], c)), i == 0, i == 1)
                    mm.then_inc(self.down, 1)

            iteration(0, True, False)
            with pe.Fori(1, FIT - 1) as it:
                iteration(it, False, False)
            iteration(FIT - 1, False, True)
            pe.wait_ge(self.tail, 2 * 4 * (self.done + FIT))
            for i in range(2):
                pe.transpose(psum[:2 * CT, 6, P * i:P * (i + 1)], tails[:, 2 * i:2 * i + 2, :].rearrange("p j t -> p (j t)"),
                             ident[:, :]).then_inc(self.tails_turned, 1)

        def pieces(self, c):
            start, n = CH[c]
            return [(start, start + n)] if c < NCH - 1 else [(start, SEQ), (SMP, TW)]

        def act(self, act, next_split, beside=lambda e, n: None):
            self.split(act, None, 0, 1)

            def value_hi(done, o):
                i, c = o // (2 * NCH), o % NCH
                start, n = CH[c]
                act.wait_ge(self.prod, 2 * NCH * done + NCH * i + c + 1)
                act.activation(h_hi[i][:, start:start + n], prod[:, k_par(c, i), :n], ACT.Copy).then_inc(self.h_hi, 1)

            def iteration(it, first, last):
                done = self.done + it
                for o in range(UP):
                    u, c = divmod(o, NCH)
                    g, i = u % 2, u // 2
                    start, n = CH[c]
                    if o in self.SPLITS and not (first and self.SPLITS[o] == 2):
                        self.split(act, None, it, self.SPLITS[o])
                    if o and (o - 1) // NCH % 2:
                        value_hi(done, o - 1)
                    if first and o == 0:
                        if self.layer == 0:
                            self.split(act, None, it, 2)
                        self.norm_in.act_roots(act)
                        self.norm_in.act_spread(act, (0, 1))
                        if self.layer == 1:
                            self.norm_in.act_spread(act, (2,))
                            self.split(act, None, it, 2)
                    if first and o == 1 and self.layer == 0:
                        self.norm_in.act_spread(act, (2,))
                    act.wait_ge(self.free, RING + UP * done + o + 1)
                    if c == 0:
                        act.wait_ge(self.cur, 2 * done + 2)
                    if c == NCH - 1:
                        act.wait_ge(self.hist, 4 * done + u + 1)
                    po = o - 2
                    if po >= 0 or not first:
                        pu = (po % UP) // NCH
                        if pu % 2:
                            before = 2 * NCH * done + (po % UP) // (2 * NCH) * NCH + po % NCH + 1
                            act.wait_ge(self.prod, before if po >= 0 else before - 2 * NCH)
                        else:
                            before = 2 * NCH * done + (po % UP) // (2 * NCH) * NCH + po % NCH + 1
                            act.wait_ge(self.silu, before)
                    act.activation(conv_t[:, o % 2, :n], a_buf[g][:, start + 2:start + 2 + n], ACT.Identity,
                                   scale=cur[:, 2, g, i:i + 1], bias=cur[:, 3, g, i:i + 1]).then_inc(self.affine, 1)
                    k = 2 * NCH * done + NCH * i + c
                    if g == 0:
                        act.wait_ge(self.conv, UP * done + o + 1)
                        act.activation(s_gate[:, start:start + n], conv_t[:, o % 2, :n], ACT.Silu).then_inc(self.silu, 1)
                value_hi(done, UP - 1)
                for n in range(DOWN):
                    c, d = divmod(n, KT)
                    if n in self.NEXT_SPLITS:
                        if not last:
                            self.split(act, None, it + 1, self.NEXT_SPLITS[n])
                        else:
                            next_split(act, None, self.NEXT_SPLITS[n])
                    if last:
                        beside(act, n)
                        self.norm_out.act_tile(act, c, d)

            iteration(0, True, False)
            with act.Fori(1, FIT - 1) as it:
                iteration(it, False, False)
            iteration(FIT - 1, False, True)
            beside(act, DOWN)
            for i in range(2):
                act.wait_ge(self.tails_turned, 2 * self.layer + 2)
                act.activation(tails_row[:2 * CT, i, :], psum[:2 * CT, 6, P * i:P * (i + 1)], ACT.Copy)\
                    .then_inc(self.tails_row, 1)

        def dve(self, dve, next_split, beside=lambda e, n: None):
            self.split(None, dve, 0, 1)

            def value_lo(done, o):
                i, c = o // (2 * NCH), o % NCH
                start, n = CH[c]
                dve.wait_ge(self.h_hi, 2 * NCH * done + NCH * i + c + 1)
                dve.tensor_tensor(h_lo[i][:, start:start + n], prod[:, k_par(c, i), :n], h_hi[i][:, start:start + n],
                                  ALU.subtract).then_inc(self.h_lo, 1)

            def iteration(it, first, last):
                done = self.done + it
                for o in range(UP):
                    u, c = divmod(o, NCH)
                    g, i = u % 2, u // 2
                    start, n = CH[c]
                    if first and o == 0:
                        if self.layer == 0:
                            self.split(None, dve, it, 2)
                        self.norm_in.dve_columns(dve)
                        if self.layer == 1:
                            self.split(None, dve, it, 2)
                    if first and u == 0:
                        self.norm_in.rstd_wait(dve, c)
                    dve.wait_ge(self.up, UP * done + o + 1)
                    if first and o in (0, NCH):
                        dve.wait_ge(self.edge, 2 * self.layer + 2)
                    for a, b in self.pieces(c):
                        mm = dve.tensor_tensor(a_buf[g][:, a + 2:b + 2], psum[:, o % RING, a - start:b - start],
                                               rstd[:, a:b], ALU.mult)
                    mm.then_inc(self.free, 1)
                    if o and (o - 1) // NCH % 2:
                        value_lo(done, o - 1)
                    t = conv_t[:, o % 2, :n]
                    dve.wait_ge(self.affine, UP * done + o + 1)
                    dve.scalar_tensor_tensor(t, a_buf[g][:, start + 1:start + 1 + n], cur[:, 1, g, i:i + 1], t,
                                             ALU.mult, ALU.add).then_inc(self.conv1, 1)
                    dve.wait_ge(self.conv1, UP * done + o + 1)
                    dve.scalar_tensor_tensor(t, a_buf[g][:, start:start + n], cur[:, 0, g, i:i + 1], t,
                                             ALU.mult, ALU.add).then_inc(self.conv, 1)
                    if g == 1:
                        k = 2 * NCH * done + NCH * i + c
                        dve.wait_ge(self.conv, UP * done + o + 1)
                        dve.wait_ge(self.silu, k + 1)
                        pr = prod[:, k_par(c, i), :n]
                        dve.tensor_tensor(pr, t, s_gate[:, start:start + n], ALU.mult).then_inc(self.prod, 1)
                    if o in self.SPLITS and not (first and self.SPLITS[o] == 2):
                        self.split(None, dve, it, self.SPLITS[o])
                value_lo(done, UP - 1)
                at_least(dve, self.added, DOWN * done)
                for n in range(DOWN):
                    c, d = divmod(n, KT)
                    if n in self.NEXT_SPLITS:
                        if not last:
                            self.split(None, dve, it + 1, self.NEXT_SPLITS[n])
                        else:
                            next_split(None, dve, self.NEXT_SPLITS[n])
                    dve.wait_ge(self.down, DOWN * done + n + 1)
                    mm = dve.tensor_tensor(chunk(x[:, d, :], c), chunk(x[:, d, :], c), psum[:, n % RING, :CH[c][1]],
                                           ALU.add)
                    mm.then_inc(self.added, 1)
                    if last and c:
                        self.norm_out.dve_tile(dve, c - 1, d)
                    if last:
                        beside(dve, n + 1)

            iteration(0, True, False)
            with dve.Fori(1, FIT - 1) as it:
                iteration(it, False, False)
            iteration(FIT - 1, False, True)
            for d in range(KT):
                self.norm_out.dve_tile(dve, NCH - 1, d)

        def pool(self, pool, region_free):
            if self.layer == 0:
                for c in range(NCH - 1):
                    self.norm_in.pool(pool, c)
            region_free(pool)
            for t in (a_gate, a_val):
                pool.memset(t[:, 0:2], 0.0).then_inc(self.edge, 1)

            def iteration(it, first, last):
                done = self.done + it
                at_least(pool, self.conv, UP * done)
                stand(pool)
                for g in range(2):
                    pool.tensor_copy(cur[:, :, g, :], taps[self.layer][:, :, bass.ds(FT * g + 2 * it, 2)])\
                        .then_inc(self.cur, 1)
                if first and self.layer == 0:
                    self.norm_in.pool(pool, NCH - 1)
                pool.wait_ge(self.cur, 2 * done + 2)
                stand(pool)
                for u in range(4):
                    g, i = u % 2, u // 2
                    if u >= 2:
                        pool.wait_ge(self.conv, UP * done + NCH * (u - 1))
                        stand(pool)
                    pool.tensor_copy(a_buf[g][:, SMP:SMP + 2], cur[:, 4:6, g, i]).then_inc(self.hist, 1)
                    pool.wait_ge(self.free, RING + UP * done + NCH * (u + 1))
                    stand(pool)
                    for r, col in enumerate((SEQ, TW)):
                        pool.tensor_copy(tails[:, 2 * r:2 * r + 2, bass.ds(FT * g + 2 * it + i, 1)],
                                         a_buf[g][:, col:col + 2].rearrange("p (j o) -> p j o", o=1))\
                            .then_inc(self.tail, 1)

            iteration(0, True, False)
            with pool.Fori(1, FIT - 1) as it:
                iteration(it, False, False)
            iteration(FIT - 1, False, True)

    def k_par(c, i):
        return (NCH * i + c) % 2

    SETS = KT // 2
    OUT6 = 2 * NCH
    g_raw = sem("g_raw")
    g_hi = sem("g_hi")
    g_lo = sem("g_lo")
    g_out = sem("g_out")
    g_free = sem("g_free")
    gelu_done = sem("gelu_done")
    v_squared = sem("v_squared")
    v_added = sem("v_added")
    ws_in = sem("ws_in")
    bs_in = sem("bs_in")
    ws_turned = sem("ws_turned")
    ws_copied = sem("ws_copied")
    g_zero = sem("g_zero")
    v_sum = sem("v_sum")
    v_mean = sem("v_mean")
    v_root = sem("v_root")
    v_rstd = sem("v_rstd")
    vt_turned = sem("vt_turned")
    vt_copied = sem("vt_copied")
    mix_done = sem("mix_done")
    mix_added = sem("mix_added")
    gated = sem("gated")
    gs_hi = sem("gs_hi")
    gs_lo = sem("gs_lo")
    g_added = sem("g_added")
    gv_out = sem("gv_out")
    HALF = CK

    def raw_unit(u):
        return raw0[:, :].rearrange("p (k i n) -> p k i n", k=KT, i=2)[:, :, u, :]

    def g_split(act, dve, i, u):
        if act is not None:
            act.wait_ge(g_raw, 16 * (i + 1))
            act.activation(w_hi[u][:, :].rearrange("p (k n) -> p k n", k=KT), raw_unit(u), ACT.Copy).then_inc(g_hi, 1)
        else:
            dve.wait_ge(g_hi, 2 * i + u + 1)
            dve.tensor_tensor(w_lo[u][:, :].rearrange("p (k n) -> p k n", k=KT), raw_unit(u),
                              w_hi[u][:, :].rearrange("p (k n) -> p k n", k=KT), ALU.subtract).then_inc(g_lo, 1)

    def g_splits(act, dve, i, o, last=False):
        if o == 1 and not (isinstance(i, int) and i == 0):
            if act is not None:
                at_least(act, g_out, OUT6 * i)
            g_split(act, dve, i, 1)
        if o == 4 and not last:
            if act is not None:
                act.wait_ge(g_out, OUT6 * i + NCH)
            g_split(act, dve, i + 1, 0)

    def g_sp(sp, region_free):
        def load(src):
            sp.dma_start(raw0[:, :].rearrange("p (k n) -> p k n", k=KT), src.rearrange("(k p) n -> p k n", p=P))\
                .then_inc(g_raw, 16)

        region_free(sp)
        sp.dma_start(vt0[:, :, :, :].rearrange("p k h n -> p (k h) n"), b_w_s[0].rearrange("g p q -> p g q"))\
            .then_inc(ws_in, 16)
        for h in range(2):
            src = bass.AP(b_bias_s.tensor, h * P, [[0, HALF], [2 * P, KT], [1, P]])
            sp.dma_start(bs[HALF * h:HALF * (h + 1), :, :], src).then_inc(bs_in, 16)
        sp.dma_start(gain_v[:, :], bass.AP(b_v_norm.tensor, 0, [[0, P], [1, D]])).then_inc(bs_in, 16)
        for i in range(1, SETS):
            sp.wait_ge(g_lo, 2 * i)
            load(b_w_in[0, :, D + 2 * P * i:D + 2 * P * (i + 1)])
        with sp.Fori(SETS, 2 * SETS) as i:
            sp.wait_ge(g_lo, 2 * i)
            stand(sp)
            load(b_w_in[0, :, bass.ds(2 * P * (i - SETS), 2 * P)])
        sp.wait_ge(vt_copied, NB + 1)
        for h in range(2):
            sp.dma_start(new_gmlp_v[0, 0].rearrange("t (k h e) -> t k h e", h=2, e=HALF)[:, :, h, :],
                         v_pad[NB % 2][:DEC, :, h, HALF * h:HALF * (h + 1)]).then_inc(gv_out, 16)
        with sp.Fori(2 * SETS, 3 * SETS) as i:
            sp.wait_ge(g_lo, 2 * i)
            stand(sp)
            load(b_w_out[0, :, bass.ds(2 * P * (i - 2 * SETS), 2 * P)])

    def g_sp_first(sp):
        sp.wait_ge(ffn[0].w_lo, WEIGHTS * FIT)
        sp.dma_start(raw0[:, :].rearrange("p (k n) -> p k n", k=KT),
                     b_w_in[0, :, D:D + 2 * P].rearrange("(k p) n -> p k n", p=P)).then_inc(g_raw, 16)

    def mixing(turn, mix):
        for b in range(NB + 3):
            if b < NB + 1:
                turn(b)
            if b >= 2:
                mix(b - 2)

    def beside_u(output, rest):
        for o in range(OUT6):
            output(o)
            if o > NCH:
                rest(o - NCH - 1, [KT - 1])
            if o >= NCH:
                rest(o - NCH, range(KT - 1))
        rest(NCH - 1, [KT - 1])

    def g_pe(pe, norm):
        def outputs(i, wait, norm=None):
            for o in range(OUT6):
                u, c = divmod(o, NCH)
                wait(o, u, c)
                if c == 0:
                    pe.wait_ge(g_lo, 2 * i + u + 1)
                pe.wait_ge(g_free, OUT6 * i + o + 1)
                linear(pe, psum[:, o, :CH[c][1]], w_hi[u], w_lo[u], c, norm if u == 0 else None).then_inc(g_out, 1)

        def first(o, u, c):
            pe.wait_ge(Ffn.added, DOWN * FIT - RING + o + 1)
            if o == 2:
                norm.pe_columns(pe)
            if o == 4:
                pe.wait_ge(Ffn.tails_row, 2)
                norm.pe_spread(pe, (0, 1))
            if o == 5:
                norm.pe_spread(pe, (2,))

        outputs(0, first, norm)
        with pe.Fori(1, SETS) as i:
            outputs(i, lambda o, u, c: None)
        pe.wait_ge(ws_in, 16)
        pe.wait_ge(Norm.c_ready, 3 * norm.nth + 3)
        for j in range(GROUPS // 4):
            at_least(pe, ws_copied, j - 1)
            for k in range(4):
                g = 4 * j + k
                mm = pe.transpose(psum[:, 6 + j % 2, P * k:P * (k + 1)], vt0[:, g // 2, g % 2, :], ident[:, :])
            mm.then_inc(ws_turned, 1)
        pe.wait_ge(v_added, NCH * KT)
        pe.wait_ge(ws_copied, GROUPS // 4)
        for b, (start, n) in enumerate(BLOCKS):
            mm = pe.matmul(psum[:n, 7, 2 * b:2 * b + 2], total[:, start:start + n], ones[:, 0:2], start=True, stop=True)
        mm.then_inc(v_sum, 1)
        pe.wait_ge(g_free, RING + OUT6 * SETS)
        pe.wait_ge(gelu_done, OUT6 * SETS)

        def turn(b):
            start, n = BLOCKS[b]
            at_least(pe, vt_copied, b - 1)
            for d in range(KT):
                mm = pe.transpose(psum[:n, 2 * (b % 2) + d // 4, P * (d % 4):P * (d % 4 + 1)],
                                  vT[:, d, start:start + n], ident[:, :])
            mm.then_inc(vt_turned, 1)

        def mix(b):
            n = BLOCKS[b][1]
            if b == 0:
                pe.wait_ge(g_zero, 3)
            pe.wait_ge(vt_copied, b + 1)
            at_least(pe, mix_added, b - 1)
            for d in range(KT):
                for h in range(2):
                    mm = pe.matmul(psum[:, 4 + 2 * (b % 2) + d // 4, P * (d % 4):P * (d % 4) + n],
                                   v_pad[b % 2][:n, d, h, :], wsT[:n, 2 * d + h, :n], start=(h == 0), stop=(h == 1))
            mm.then_inc(mix_done, 1)

        mixing(turn, mix)
        pe.wait_ge(mix_added, NB + 1)
        with pe.Fori(SETS, 2 * SETS) as i:
            outputs(i, lambda o, u, c: None)
        with pe.Fori(2 * SETS, 3 * SETS) as i:
            outputs(i, lambda o, u, c: pe.wait_ge(gs_lo, KT * (c + 1)))

    def g_act(act, norm, norm_out):
        def v_set(i, first):
            for o in range(OUT6):
                u, c = divmod(o, NCH)
                n = CH[c][1]
                if first and o == 0:
                    norm.act_roots(act)
                    norm.act_spread(act, (0, 1))
                if first and o == 2:
                    norm.act_spread(act, (2,))
                g_splits(act, None, i, o)
                act.wait_ge(g_free, RING + OUT6 * i + o + 1)
                if not first:
                    stand(act)
                dst = chunk(vT, c)[:, 2 * i + u, :] if isinstance(i, int) else chunk(vT, c)[:, bass.ds(2 * i + u, 1), :]
                src = gm_t[:, o % 2, :n] if isinstance(i, int) else gm_t[:, o % 2:o % 2 + 1, :n]
                act.activation(dst, src, ACT.Gelu).then_inc(gelu_done, 1)
                if first and o < 2:
                    act.wait_ge(Norm.added, norm.tiles + NCH * KT)
                else:
                    act.wait_ge(v_added, OUT6 * i + o - 1)
                act.wait_ge(gelu_done, OUT6 * i + o + 1)
                if not first:
                    stand(act)
                sq = squares[:, o % 2, :n] if isinstance(i, int) else squares[:, o % 2:o % 2 + 1, :n]
                act.activation(sq, dst, ACT.Square).then_inc(v_squared, 1)

        v_set(0, True)
        with act.Fori(1, SETS) as i:
            v_set(i, False)
        for j in range(GROUPS // 4):
            act.wait_ge(ws_turned, j + 1)
            act.activation(wsT[:, 4 * j:4 * j + 4, :].rearrange("p g n -> p (g n)"), psum[:, 6 + j % 2, :],
                           ACT.Copy).then_inc(ws_copied, 1)
        act.wait_ge(v_mean, 2)
        act.activation(rc_v[:, :NB], rc_v[:, :NB], ACT.Sqrt).then_inc(v_root, 1)
        act.activation(rc_v[:DEC, NB:], rc_v[:DEC, NB:], ACT.Sqrt).then_inc(v_root, 1)
        def u_output(i, o):
            n = CH[o % NCH][1]
            g_splits(act, None, i, o)
            act.wait_ge(g_free, RING + OUT6 * i + o + 1)
            act.activation(gm_t[:, o % 2, :n], gm_t[:, o % 2, :n], ACT.Gelu).then_inc(gelu_done, 1)

        def gated_hi(c, tiles):
            for d in tiles:
                if d == 0:
                    act.wait_ge(g_out, OUT6 * 2 * SETS - NCH + c + 1)
                    act.wait_ge(gated, 2 + NCH * (KT - 1))
                if d == KT - 1:
                    act.wait_ge(gated, 2 + NCH * (KT - 1) + c + 1)
                act.activation(chunk(gx_hi[:, d, :], c), chunk(vT[:, d, :], c), ACT.Copy).then_inc(gs_hi, 1)

        with act.Fori(SETS, 2 * SETS - 1) as i:
            for o in range(OUT6):
                u_output(i, o)
        beside_u(lambda o: u_output(2 * SETS - 1, o), gated_hi)

        def square(i, o):
            u, c = divmod(o, NCH)
            k = OUT6 * (i - 2 * SETS) + o
            act.wait_ge(g_free, RING + OUT6 * i + o + 1)
            act.wait_ge(Norm.added, norm_out.tiles + k - 1)
            if not isinstance(i, int):
                stand(act)
            act.activation(squares[:, o % 2:o % 2 + 1, :CH[c][1]],
                           chunk(x, c)[:, bass.ds(2 * (i - 2 * SETS) + u, 1), :], ACT.Square).then_inc(Norm.squared, 1)

        act.wait_ge(v_added, NCH * KT)
        with act.Fori(2 * SETS, 3 * SETS - 1) as i:
            for o in range(OUT6):
                g_splits(act, None, i, o)
                square(i, o)
        i = 3 * SETS - 1
        for o in range(OUT6):
            u, c = divmod(o, NCH)
            g_splits(act, None, i, o, True)
            if o == 4:
                act.wait_ge(g_out, OUT6 * i + NCH)
                ffn[1].split(act, None, 0, 0)
            square(i, o)
            if u == 1:
                for d in range(KT):
                    norm_out.act_hi(act, c, d)

    def g_dve(dve, norm, norm_out):
        def to_buffer(i, o):
            start, n = CH[o % NCH]
            dve.wait_ge(g_out, OUT6 * i + o + 1)
            dve.tensor_tensor(gm_t[:, o % 2, :n], psum[:, o, :n], rstd[:, start:start + n], ALU.mult).then_inc(g_free, 1)

        def v_set(i, first):
            for o in range(OUT6):
                if first and o == 0:
                    norm.dve_columns(dve)
                if first and o < NCH:
                    norm.rstd_wait(dve, o)
                g_splits(None, dve, i, o)
                if not first or o >= 2:
                    dve.wait_ge(gelu_done, OUT6 * i + o - 1)
                elif o == 0:
                    dve.wait_ge(ws_in, 16)
                to_buffer(i, o)

        v_set(0, True)
        with dve.Fori(1, SETS) as i:
            v_set(i, False)
        dve.wait_ge(v_sum, 1)
        sums = psum[:, 7, :2 * (NB + 1)].rearrange("p (b i) -> p b i", i=2)
        for rows, cut in ((slice(0, P), slice(0, NB)), (slice(0, DEC), slice(NB, NB + 1))):
            dve.tensor_scalar(rc_v[rows, cut], sums[rows, cut, 0], 1.0 / D, EPS, ALU.mult, ALU.add).then_inc(v_mean, 1)
        for k, (rows, cut) in enumerate(((slice(0, P), slice(0, NB)), (slice(0, DEC), slice(NB, NB + 1)))):
            dve.wait_ge(v_root, k + 1)
            dve.reciprocal(rc_v[rows, cut], rc_v[rows, cut]).then_inc(v_rstd, 1)
        dve.wait_ge(v_rstd, 2)
        dve.wait_ge(bs_in, 48)
        dve.wait_ge(g_zero, 2)

        def turn(b):
            n = BLOCKS[b][1]
            dve.wait_ge(vt_turned, b + 1)
            at_least(dve, mix_done, b - 1)
            for bank in range(2):
                src = psum[:n, 2 * (b % 2) + bank, :].rearrange("p (k h e) -> p k h e", h=2, e=HALF)
                g = gain_v[:n, :].rearrange("p (k h e) -> p k h e", h=2, e=HALF)[:, 4 * bank:4 * bank + 4]
                for h in range(2):
                    mm = dve.scalar_tensor_tensor(v_pad[b % 2][:n, 4 * bank:4 * bank + 4, h, HALF * h:HALF * (h + 1)],
                                                  src[:, :, h, :], rc_v[:n, b:b + 1], g[:, :, h, :], ALU.mult, ALU.mult)
            mm.then_inc(vt_copied, 1)

        def mix(b):
            start, n = BLOCKS[b]
            dve.wait_ge(mix_done, b + 1)
            for bank in range(2):
                src = psum[:, 4 + 2 * (b % 2) + bank, :].rearrange("p (k n) -> p k n", n=P)[:, :, :n]
                mm = dve.tensor_tensor(vT[:, 4 * bank:4 * bank + 4, start:start + n], src,
                                       bs[:, 4 * bank:4 * bank + 4, :n], ALU.add)
            mm.then_inc(mix_added, 1)

        mixing(turn, mix)
        def u_output(i, o):
            g_splits(None, dve, i, o)
            dve.wait_ge(gated, OUT6 * (i - SETS) + o + 1)
            to_buffer(i, o)

        def gated_lo(c, tiles):
            for d in tiles:
                dve.wait_ge(gs_hi, KT * c + d + 1)
                dve.tensor_tensor(chunk(gx_lo[:, d, :], c), chunk(vT[:, d, :], c), chunk(gx_hi[:, d, :], c),
                                  ALU.subtract).then_inc(gs_lo, 1)

        with dve.Fori(SETS, 2 * SETS - 1) as i:
            for o in range(OUT6):
                u_output(i, o)
        beside_u(lambda o: u_output(2 * SETS - 1, o), gated_lo)

        def w_out_set(i, last):
            for o in range(OUT6):
                u, c = divmod(o, NCH)
                g_splits(None, dve, i, o, last)
                dve.wait_ge(g_out, OUT6 * i + o + 1)
                tile = chunk(x, c)[:, bass.ds(2 * (i - 2 * SETS) + u, 1), :]
                mm = dve.tensor_tensor(tile, tile, psum[:, o:o + 1, :CH[c][1]], ALU.add)
                mm.then_inc(g_free, 1)
                if last and o == 4:
                    ffn[1].split(None, dve, 0, 0)
                if last and o >= 4:
                    for d in range(KT):
                        norm_out.dve_tile(dve, c - 1, d)

        with dve.Fori(2 * SETS, 3 * SETS - 1) as i:
            w_out_set(i, False)
        w_out_set(3 * SETS - 1, True)
        for d in range(KT):
            norm_out.dve_tile(dve, NCH - 1, d)

    def g_pool(pool, norm, norm_out, region_free):
        for c in range(NCH):
            norm.pool(pool, c)

        def sums(i, first):
            for o in range(OUT6):
                u, c = divmod(o, NCH)
                k = OUT6 * i + o
                sq = squares[:, o % 2, :CH[c][1]]
                pool.wait_ge(v_squared, k + 1)
                if first and u == 0:
                    pool.wait_ge(Norm.c_ready, 3 * norm.nth + 3)
                    pool.tensor_copy(chunk(total, c), sq).then_inc(v_added, 1)
                else:
                    pool.wait_ge(v_added, k - NCH + 1)
                    pool.tensor_tensor(chunk(total, c), chunk(total, c), sq, ALU.add).then_inc(v_added, 1)

        sums(0, True)
        pool.wait_ge(ws_in, 16)
        pool.memset(vt1[:, :, :, :], 0.0).then_inc(g_zero, 1)
        with pool.Fori(1, SETS) as i:
            sums(i, False)
        pool.wait_ge(ws_copied, GROUPS // 4)
        pool.memset(vt0[:, :, :, :], 0.0).then_inc(g_zero, 1)
        pool.wait_ge(g_zero, 2)
        pool.memset(wsT[CK:, :, :CK], 0.0).then_inc(g_zero, 1)
        pool.wait_ge(g_zero, 3)
        pool.sem_inc(gated, 2)
        pool.wait_ge(mix_added, NB + 1)
        with pool.Fori(SETS, 2 * SETS) as i:
            for o in range(OUT6):
                u, c = divmod(o, NCH)
                pool.wait_ge(gelu_done, OUT6 * i + o + 1)
                tile = chunk(vT, c)[:, bass.ds(2 * (i - SETS) + u, 1), :]
                pool.tensor_tensor(tile, tile, gm_t[:, o % 2:o % 2 + 1, :CH[c][1]], ALU.mult).then_inc(gated, 1)

        def next_sums(i, first):
            for o in range(OUT6):
                c = o % NCH
                k = norm_out.tiles + OUT6 * (i - 2 * SETS) + o
                sq = squares[:, o % 2, :CH[c][1]]
                pool.wait_ge(Norm.squared, k + 1)
                if first and o < NCH:
                    pool.tensor_copy(chunk(total, c), sq).then_inc(Norm.added, 1)
                else:
                    pool.wait_ge(Norm.added, k - NCH + 1)
                    pool.tensor_tensor(chunk(total, c), chunk(total, c), sq, ALU.add).then_inc(Norm.added, 1)

        pool.wait_ge(v_sum, 1)
        next_sums(2 * SETS, True)
        with pool.Fori(2 * SETS + 1, 3 * SETS) as i:
            next_sums(i, False)

    fg_in = sem("fg_in")
    y_sum = sem("y_sum")
    y_mean = sem("y_mean")
    y_root = sem("y_root")
    y_rstd = sem("y_rstd")
    y_turned = sem("y_turned")
    y_done = sem("y_done")
    y_out = [sem(f"y_out{i}") for i in range(3)]
    EARLY = CH[-1][0] // P
    BESIDE = DOWN - 1
    Y_COLS = [(slice(0, P), slice(0, EARLY)), (slice(0, P), slice(EARLY, NB)), (slice(0, DEC), slice(NB, NB + 1))]
    Y_GROUPS = [(range(EARLY), Y_COLS[:1]), (range(EARLY, NB + 1), Y_COLS[1:])]

    def y_sums(pe, group):
        pe.wait_ge(Norm.added, norm_e.tiles + KT * (NCH - 1 + group))
        for b in Y_GROUPS[group][0]:
            start, n = BLOCKS[b]
            mm = pe.matmul(psum[:n, 7, 2 * b:2 * b + 2], total[:, start:start + n], ones[:, 0:2], start=True, stop=True)
        mm.then_inc(y_sum, 1)

    def y_turn(pe, b):
        start, n = BLOCKS[b]
        if b < 3:
            pe.wait_ge(Ffn.added, DEPTH * DOWN * FIT - RING + 2 * b + 2)
        else:
            pe.wait_ge(y_done, b - 2)
        if b == EARLY:
            pe.wait_ge(Ffn.added, DEPTH * DOWN * FIT)
        for d in range(KT):
            mm = pe.transpose(psum[:n, 2 * (b % 3) + d // 4, P * (d % 4):P * (d % 4 + 1)],
                              x[:, d, start:start + n], ident[:, :])
        mm.then_inc(y_turned, 1)

    def y_roots(act, group):
        for k, (rows, cut) in enumerate(Y_GROUPS[group][1]):
            act.wait_ge(y_mean, group + k + 1)
            act.activation(rs_col[rows, cut], rs_col[rows, cut], ACT.Sqrt).then_inc(y_root, 1)

    def y_means(dve, group):
        dve.wait_ge(y_sum, group + 1)
        sums = psum[:, 7, :2 * (NB + 1)].rearrange("p (b i) -> p b i", i=2)
        for rows, cut in Y_GROUPS[group][1]:
            dve.tensor_scalar(rs_col[rows, cut], sums[rows, cut, 0], 1.0 / D, EPS, ALU.mult, ALU.add)\
                .then_inc(y_mean, 1)

    def y_inverse(dve, group):
        for k, (rows, cut) in enumerate(Y_GROUPS[group][1]):
            dve.wait_ge(y_root, group + k + 1)
            dve.reciprocal(rs_col[rows, cut], rs_col[rows, cut]).then_inc(y_rstd, 1)
        dve.wait_ge(y_rstd, group + len(Y_GROUPS[group][1]))

    def y_block(dve, b):
        n = BLOCKS[b][1]
        dve.wait_ge(y_turned, b + 1)
        at_least(dve, y_out[b % 3], 16 * (b // 3))
        for i in range(2):
            cut = slice(BANK * i, BANK * (i + 1))
            mm = dve.scalar_tensor_tensor(y_tile[b % 3][:n, cut], psum[:n, 2 * (b % 3) + i, :], rs_col[:n, b:b + 1],
                                          final_g[:n, cut], ALU.mult, ALU.mult)
        mm.then_inc(y_done, 1)

    def beside_pe(pe, n):
        if n == BESIDE:
            y_sums(pe, 0)

    def beside_act(act, n):
        if n == DOWN:
            y_roots(act, 0)

    def beside_dve(dve, n):
        if n == BESIDE + 1:
            y_means(dve, 0)

    def final_pe(pe):
        for b in range(NB + 1):
            if b == 2:
                pe.wait_ge(y_mean, 1)
                y_sums(pe, 1)
            y_turn(pe, b)

    def final_act(act):
        y_roots(act, 1)

    def final_dve(dve):
        dve.wait_ge(fg_in, 16)
        y_inverse(dve, 0)
        for b in range(NB + 1):
            if b == 1:
                y_means(dve, 1)
            if b == 2:
                y_inverse(dve, 1)
            y_block(dve, b)

    def store_blocks(sp, blocks):
        for b in blocks:
            start, n = BLOCKS[b]
            sp.wait_ge(y_done, b + 1)
            dst = y_prompt[0, start:start + n, :] if b < NB else y_sample[0]
            sp.dma_start(dst, y_tile[b % 3][:n, :]).then_inc(y_out[b % 3], 16)

    def final_sp_first(sp):
        sp.wait_ge(ffn[1].w_lo, WEIGHTS * (2 * FIT - 1) + 4)
        sp.dma_start(final_g[:, :], bass.AP(ln_final.tensor, 0, [[0, P], [1, D]])).then_inc(fg_in, 16)

    def final_sp(sp):
        store_blocks(sp, range(NB + 1))

    def attention_over(engine):
        engine.wait_ge(at_added, 1 + BURST * PAIRS)
        engine.wait_ge(k_out, 32 * PAIRS)
        engine.wait_ge(v_out, 32 * PAIRS)

    def w_o_banks_free(pe, o):
        if o < 4:
            pe.wait_ge(at_added, 1 + BURST * PAIRS - 4 + o + 1)
        else:
            pe.wait_ge(t_free, 2 + T_FIRST + T_PAIR * (PAIRS - 1) + PV_PAIR)

    def ffn0_over(engine):
        engine.wait_ge(ffn[0].added, DOWN * FIT)
        engine.wait_ge(ffn[0].tails_out, 32)

    def gmlp_over(engine):
        engine.wait_ge(gs_lo, NCH * KT)
        engine.wait_ge(gv_out, 32)

    ffn = []
    norm_b = Norm(1, 2, lambda e, c, d: e.wait_ge(at_added, 1 + BURST * (PAIRS - 1) + KT * c + d + 1))
    norm_c = Norm(2, 1, lambda e, c, d: e.wait_ge(ffn[0].added, DOWN * (FIT - 1) + KT * c + d + 1))
    norm_d = Norm(3, 3, None)
    norm_e = Norm(4, 4, lambda e, c, d: e.wait_ge(ffn[1].added, DOWN * (2 * FIT - 1) + KT * c + d + 1), split=False)
    ffn.append(Ffn(0, norm_b, norm_c))
    ffn.append(Ffn(1, norm_d, norm_e))

    block = ctx.enter_context(nc.Block())

    @block.sync
    def _(sp):
        input_sp(sp)
        attention_first_sp(sp)
        attention_second_sp(sp)
        attention_sp(sp)
        sp.wait_ge(at_lo, 4 * PAIRS)
        ffn[0].sp_first(sp)
        ffn[0].sp(sp, attention_over, g_sp_first)
        g_sp(sp, ffn0_over)
        sp.wait_ge(g_lo, 2 * 3 * SETS)
        ffn[1].sp_first(sp)
        ffn[1].sp(sp, gmlp_over, final_sp_first)
        final_sp(sp)
        for semaphore, stores in ((k_out, 2 * PAIRS), (v_out, 2 * PAIRS), (gv_out, 2), (Ffn.tails_out, 2 * DEPTH),
                                  (y_out[0], 3), (y_out[1], 3), (y_out[2], 3)):
            sp.wait_ge(semaphore, 16 * stores)

    @block.gpsimd
    def _(pool):
        input_pool(pool)
        for c in range(NCH):
            norm_a.pool(pool, c)
        attention_pool(pool)
        ffn[0].pool(pool, attention_over)
        g_pool(pool, norm_c, norm_d, ffn0_over)
        ffn[1].pool(pool, gmlp_over)
        for c in range(NCH):
            pool.wait_ge(Norm.c_ready, 3 * norm_d.nth + 3)
            norm_e.pool(pool, c)

    @block.scalar
    def _(act):
        act.sem_inc(t_free, 2)
        input_act_dma(act)
        input_act(act)
        attention_act(act, norm_b)
        ffn[0].act(act, lambda a, d, u: g_split(a, d, 0, u))
        g_act(act, norm_c, norm_d)
        act.wait_ge(g_out, OUT6 * 3 * SETS)
        ffn[1].act(act, lambda a, d, u: None, beside_act)
        final_act(act)

    @block.tensor
    def _(pe):
        pe.sem_inc(pv_done, 1)
        pe.sem_inc(wo_done, 1)
        input_pe(pe)
        attention_pe(pe)
        ffn[0].pe(pe, w_o_banks_free)
        g_pe(pe, norm_c)
        ffn[1].pe(pe,
                  lambda e, o: e.wait_ge(g_free, RING + 3 * SETS * OUT6 - RING + o + 1), beside_pe)
        final_pe(pe)

    @block.vector
    def _(dve):
        dve.sem_inc(oq_free, 2)
        dve.sem_inc(at_added, 1)
        dve.sem_inc(Ffn.free, RING)
        dve.sem_inc(g_free, RING)
        input_dve(dve)
        attention_dve(dve, norm_b)
        ffn[0].dve(dve, lambda a, d, u: g_split(a, d, 0, u))
        g_dve(dve, norm_c, norm_d)
        ffn[1].dve(dve, lambda a, d, u: None, beside_dve)
        final_dve(dve)

    ctx.close()


INPUTS = ["x_prompt", "x_sample", "cache_a_k", "cache_a_v", "state_ffn_conv", "ln_mix", "ln_ffn", "ln_final",
          "a_w_qkv", "a_rel_bias", "a_w_o", "b_w_in", "b_v_norm", "b_w_s", "b_bias_s", "b_w_out",
          "f_w_up", "f_conv_w", "f_conv_b", "f_w_down"]


def kernel(**inputs):
    import numpy as np
    import concourse.bacc as bacc
    from concourse.bass_utils import run_bass_kernel_spmd

    nc = bacc.Bacc("TRN2", target_bir_lowering=False, num_devices=1)
    arrays, args = {}, []
    for name in INPUTS:
        a = np.ascontiguousarray(inputs[name])
        arrays[f"in_{name}"] = a
        args.append(nc.dram_tensor(f"in_{name}", a.shape, mybir.dt.from_np(a.dtype), kind="ExternalInput").ap())
    (b, seq, d), (db, dec, _) = inputs["x_prompt"].shape, inputs["x_sample"].shape
    n_a, _, past, heads, hd = inputs["cache_a_k"].shape
    depth, ff2 = inputs["f_conv_b"].shape
    n_b = inputs["b_v_norm"].shape[0]
    keep = min(512, seq)
    shapes = [(b, seq, d), (db, dec, d), (n_a, b, keep, heads, hd), (n_a, b, keep, heads, hd),
              (n_a, db, dec, heads, hd), (n_a, db, dec, heads, hd), (n_b, db, dec, inputs["b_v_norm"].shape[1]),
              (depth, b, 2, ff2), (depth, db, 2, ff2)]
    for i, shape in enumerate(shapes):
        args.append(nc.dram_tensor(f"out_{i}", shape, F32, kind="ExternalOutput").ap())
    build(nc, *args)
    r = run_bass_kernel_spmd(nc, [arrays], core_ids=[0])
    return tuple(r.results[0][f"out_{i}"] for i in range(len(shapes)))
```
